# Optimizing a Trainium2 kernel written in Bass

```python
import jax, jax.numpy as jnp
from jax import lax
import numpy as np
import math
import jax
import jax.numpy as jnp

D_MODEL = 1024
BATCH = 1
SEQ = 256
DEPTH = 2

GRID_W = 64
CTX_LEN = 256
EPS = 1e-6
F_FLOOR = 1e-20
N_MOD = 6
HG_WIDTH = 512
HG_HEADS = 4
HG_DIM = HG_WIDTH // HG_HEADS
CHUNK = 16
SC_WIDTH = 512
SC_HALF = SC_WIDTH // 2
CONV_W = 3
IN_COLS = 5 * HG_WIDTH + 3 * SC_WIDTH
SPLITS = tuple(HG_WIDTH * i for i in range(1, 6)) + (5 * HG_WIDTH + SC_WIDTH, 5 * HG_WIDTH + 2 * SC_WIDTH)
PEER_HEADS = 8
PEER_QDIM = 256
PEER_HALF = PEER_QDIM // 2
N_KEYS = 128
N_EXPERTS = N_KEYS * N_KEYS
PEER_TOPK = 16
PEER_BLOCK = 128


def rms_norm(x, g):
    xf = x.astype(jnp.float32)
    y = xf * lax.rsqrt(jnp.mean(xf * xf, axis=-1, keepdims=True) + EPS)
    return (y * g.astype(jnp.float32)).astype(x.dtype)

def modulate(h, shift, scale):
    return h * (1 + scale) + shift

def to_heads(a):
    return a.reshape(a.shape[0], a.shape[1], HG_HEADS, HG_DIM).astype(jnp.float32)

def flip(a):
    return a[:, ::-1]

def forget_terms(z, lb):
    f = lb + (1.0 - lb) * jax.nn.sigmoid(z)
    logf = jnp.log(jnp.maximum(f, F_FLOOR))
    key = (1.0 - lb) * jax.nn.sigmoid(-z)
    return logf, key

def gla_chunk(q, k, v, logf, s0):
    bsz, t, h, _ = q.shape
    dv = v.shape[-1]
    n = t // CHUNK
    q, k, v, logf = (a.reshape(bsz, n, CHUNK, h, a.shape[-1]) for a in (q, k, v, logf))
    b = jnp.cumsum(logf, axis=2)
    mask = jnp.tril(jnp.ones((CHUNK, CHUNK), bool))[None, None, :, :, None, None]
    diff = b[:, :, :, None] - b[:, :, None, :]
    decay = jnp.where(mask, jnp.exp(jnp.where(mask, diff, 0.0)), 0.0)
    att = jnp.einsum('bnthk,bntshk,bnshk->bnhts', q, decay, k)
    o_intra = jnp.einsum('bnhts,bnshv->bnthv', att, v)
    b_last = b[:, :, -1]
    q_in = q * jnp.exp(b)
    k_out = k * jnp.exp(b_last[:, :, None] - b)

    def step(s, xs):
        qc, kc, vc, dc = xs
        o = jnp.einsum('bchk,bhkv->bchv', qc, s)
        s = dc[..., None] * s + jnp.einsum('bchk,bchv->bhkv', kc, vc)
        return s, o

    xs = tuple(jnp.moveaxis(a, 1, 0) for a in (q_in, k_out, v, jnp.exp(b_last)))
    s_final, o_inter = lax.scan(step, s0, xs)
    o = o_intra + jnp.moveaxis(o_inter, 0, 1)
    return o.reshape(bsz, t, h, dv), s_final

def gla_final_state(k, v, logf):
    b = jnp.cumsum(logf, axis=1)
    kd = k * jnp.exp(b[:, -1:] - b)
    return jnp.einsum('bthk,bthv->bhkv', kd, v)

def hgrn2_mix(q, iv, zf, zb, g, lbf, lbb, s0f, s0b):
    q, iv, zf, zb = (to_heads(a) for a in (q, iv, zf, zb))
    logf_f, k_f = forget_terms(zf, lbf)
    o_f, s_f = gla_chunk(q, k_f, iv, logf_f, s0f)
    logf_b, k_b = forget_terms(zb, lbb)
    o_b, s_b = gla_chunk(flip(q), flip(k_b), flip(iv), flip(logf_b), s0b)
    o = o_f + flip(o_b)
    o = o * lax.rsqrt(jnp.mean(o * o, axis=-1, keepdims=True) + EPS)
    o = o.reshape(g.shape).astype(g.dtype) * jax.nn.silu(g)
    return o, s_f, s_b

def hgrn2_final_states(iv, zf, zb, lbf, lbb):
    iv, zf, zb = (to_heads(a) for a in (iv, zf, zb))
    logf_f, k_f = forget_terms(zf, lbf)
    s_f = gla_final_state(k_f, iv, logf_f)
    logf_b, k_b = forget_terms(zb, lbb)
    s_b = gla_final_state(flip(k_b), flip(iv), flip(logf_b))
    return s_f, s_b

def conv3(u, w, axis):
    n = u.shape[axis]
    pad = [(0, 0)] * u.ndim
    pad[axis] = (1, 1)
    up = jnp.pad(u, pad)
    return (w[0] * lax.slice_in_dim(up, 0, n, axis=axis)
            + w[1] * lax.slice_in_dim(up, 1, n + 1, axis=axis)
            + w[2] * lax.slice_in_dim(up, 2, n + 2, axis=axis))

def grid_conv(u, w, rows):
    bsz, t, ch = u.shape
    grid = u.reshape(bsz, rows, GRID_W, ch)
    horiz = conv3(grid[..., :SC_HALF], w[:, :SC_HALF], axis=2)
    vert = conv3(grid[..., SC_HALF:], w[:, SC_HALF:], axis=1)
    return jnp.concatenate([horiz, vert], axis=-1).reshape(bsz, t, ch)

def seq_conv(u, w):
    return conv3(u, w, axis=1)

def token_mixer(h, w_in_l, w_out_l, conv_w_l, lbf, lbb, s0f, s0b, conv_fn):
    iv, zf, zb, q, g, cg, bg, hv = jnp.split(h @ w_in_l, SPLITS, axis=-1)
    o_rec, s_f, s_b = hgrn2_mix(q, iv, zf, zb, g, lbf, lbb, s0f, s0b)
    o_conv = bg * conv_fn(cg * hv, conv_w_l)
    y = jnp.concatenate([o_rec, o_conv], axis=-1) @ w_out_l
    return y, s_f, s_b

def peer_ffn(h, wq, subkeys, u, v):
    bsz, t, d = h.shape
    qr = (h @ wq).astype(jnp.float32).reshape(bsz, t, PEER_HEADS, 2, PEER_HALF)
    scores = jnp.einsum('bthpd,hpkd->bthpk', qr, subkeys.astype(jnp.float32))
    s1, i1 = lax.top_k(scores[..., 0, :], PEER_TOPK)
    s2, i2 = lax.top_k(scores[..., 1, :], PEER_TOPK)
    n_cand = PEER_TOPK * PEER_TOPK
    cand = (s1[..., :, None] + s2[..., None, :]).reshape(bsz, t, PEER_HEADS, n_cand)
    cidx = (i1[..., :, None] * N_KEYS + i2[..., None, :]).reshape(bsz, t, PEER_HEADS, n_cand)
    top, pos = lax.top_k(cand, PEER_TOPK)
    eidx = jnp.take_along_axis(cidx, pos, axis=-1)
    gate = jax.nn.softmax(top, axis=-1).astype(h.dtype)
    n_blk = bsz * t // PEER_BLOCK
    n_sel = PEER_HEADS * PEER_TOPK
    hb = h.reshape(n_blk, PEER_BLOCK, d)
    eb = eidx.reshape(n_blk, PEER_BLOCK, n_sel)
    gb = gate.reshape(n_blk, PEER_BLOCK, n_sel)

    def block(args):
        hk, ek, gk = args
        act = jax.nn.gelu(jnp.einsum('ted,td->te', u[ek], hk), approximate=False)
        return jnp.einsum('te,ted->td', gk * act, v[ek])

    return lax.map(block, (hb, eb, gb)).reshape(bsz, t, d)

def first_inputs(seed: int = 0) -> dict:
    key = jax.random.key(seed)
    ks = jax.random.split(key, 17)
    nrm = lambda k, shape, scale: jax.random.normal(k, shape, jnp.float32) * scale
    mix_w = HG_WIDTH + SC_WIDTH
    return {
        'x': nrm(ks[0], (BATCH, SEQ, D_MODEL), 1.0),
        'c': nrm(ks[1], (BATCH, D_MODEL), 1.0),
        'ctx': nrm(ks[2], (BATCH, CTX_LEN, D_MODEL), 1.0),
        'c_ctx': nrm(ks[3], (D_MODEL,), 1.0),
        'w_mod': nrm(ks[4], (DEPTH, D_MODEL, N_MOD * D_MODEL), 0.5 * D_MODEL ** -0.5),
        'b_mod': nrm(ks[5], (DEPTH, N_MOD * D_MODEL), 0.01),
        'norm1_g': 1.0 + nrm(ks[6], (DEPTH, D_MODEL), 0.1),
        'norm2_g': 1.0 + nrm(ks[7], (DEPTH, D_MODEL), 0.1),
        'w_in': nrm(ks[8], (DEPTH, D_MODEL, IN_COLS), D_MODEL ** -0.5),
        'conv_w': nrm(ks[9], (DEPTH, CONV_W, SC_WIDTH), CONV_W ** -0.5),
        'w_out': nrm(ks[10], (DEPTH, mix_w, D_MODEL), mix_w ** -0.5),
        'lb_logits': nrm(ks[11], (DEPTH, 2, HG_WIDTH), 0.5),
        'peer_wq': nrm(ks[12], (DEPTH, D_MODEL, PEER_HEADS * PEER_QDIM), D_MODEL ** -0.5),
        'peer_subkeys': nrm(ks[13], (DEPTH, PEER_HEADS, 2, N_KEYS, PEER_HALF), PEER_HALF ** -0.5),
        'peer_u': nrm(ks[14], (DEPTH, N_EXPERTS, D_MODEL), D_MODEL ** -0.5),
        'peer_v': nrm(ks[15], (DEPTH, N_EXPERTS, D_MODEL), PEER_HEADS ** -0.5),
        'final_g': 1.0 + nrm(ks[16], (D_MODEL,), 0.1),
    }

def first_block(x, c, ctx, c_ctx, w_mod, b_mod, norm1_g, norm2_g, w_in, conv_w, w_out,
              lb_logits, peer_wq, peer_subkeys, peer_u, peer_v, final_g):
    rows = x.shape[1] // GRID_W
    p_lb = jax.nn.softmax(lb_logits.astype(jnp.float32), axis=0)
    lower = jnp.cumsum(p_lb, axis=0) - p_lb[0]
    cond_x = jax.nn.silu(c)
    cond_c = jax.nn.silu(c_ctx)
    latent_conv = lambda u, w: grid_conv(u, w, rows)
    zero_state = jnp.zeros((ctx.shape[0], HG_HEADS, HG_DIM, HG_DIM), jnp.float32)
    xc = ctx
    for l in range(DEPTH):
        lbf = lower[l, 0].reshape(HG_HEADS, HG_DIM)
        lbb = lower[l, 1].reshape(HG_HEADS, HG_DIM)
        mod_x = (cond_x @ w_mod[l] + b_mod[l])[:, None, :]
        mod_c = (cond_c @ w_mod[l] + b_mod[l])[None, None, :]
        sh1x, sc1x, g1x, sh2x, sc2x, g2x = jnp.split(mod_x, N_MOD, axis=-1)
        sh1c, sc1c, g1c, sh2c, sc2c, g2c = jnp.split(mod_c, N_MOD, axis=-1)
        hc = modulate(rms_norm(xc, norm1_g[l]), sh1c, sc1c)
        if l < DEPTH - 1:
            yc, s_f, s_b = token_mixer(hc, w_in[l], w_out[l], conv_w[l], lbf, lbb,
                                       zero_state, zero_state, seq_conv)
            xc = xc + g1c * yc
            hc2 = modulate(rms_norm(xc, norm2_g[l]), sh2c, sc2c)
            xc = xc + g2c * peer_ffn(hc2, peer_wq[l], peer_subkeys[l], peer_u[l], peer_v[l])
        else:
            iv_c, zf_c, zb_c = jnp.split(hc @ w_in[l][:, :3 * HG_WIDTH], 3, axis=-1)
            s_f, s_b = hgrn2_final_states(iv_c, zf_c, zb_c, lbf, lbb)
        hx = modulate(rms_norm(x, norm1_g[l]), sh1x, sc1x)
        yx, _, _ = token_mixer(hx, w_in[l], w_out[l], conv_w[l], lbf, lbb, s_f, s_b, latent_conv)
        x = x + g1x * yx
        hx2 = modulate(rms_norm(x, norm2_g[l]), sh2x, sc2x)
        x = x + g2x * peer_ffn(hx2, peer_wq[l], peer_subkeys[l], peer_u[l], peer_v[l])
    return rms_norm(x, final_g)


N_MIXERS = 3
N_LAYERS_A = (DEPTH + 2) // N_MIXERS
N_LAYERS_B = (DEPTH + 1) // N_MIXERS
N_LAYERS_C = DEPTH // N_MIXERS
HEAD_DIM = 64
N_HEADS = D_MODEL // (2 * HEAD_DIM)
V_HEAD_DIM = 2 * HEAD_DIM
Q_BLOCK = 128
ROPE_THETA = 10000.0
D_FF = 4 * D_MODEL
HYENA_EMB_DIM = 33
HYENA_FILTER_ORDER = 64
HYENA_SHORT_WIDTH = 3
HYENA_DECAY_TARGET = 1e-2
HYENA_FAST_DECAY_PCT = 0.3
HYENA_SLOW_DECAY_PCT = 1.5
CONV_WIDTH = 31
NORM_EPS = 1e-6
LN_EPS = 1e-5


def rms_norm_2(x, g, eps=NORM_EPS):
    xf = x.astype(jnp.float32)
    y = xf * lax.rsqrt(jnp.mean(xf * xf, axis=-1, keepdims=True) + eps)
    return (y * g.astype(jnp.float32)).astype(x.dtype)

def layer_norm(x, g, b, eps=LN_EPS):
    xf = x.astype(jnp.float32)
    mu = jnp.mean(xf, axis=-1, keepdims=True)
    var = jnp.mean(jnp.square(xf - mu), axis=-1, keepdims=True)
    y = (xf - mu) * lax.rsqrt(var + eps)
    return (y * g.astype(jnp.float32) + b.astype(jnp.float32)).astype(x.dtype)

def modulate_2(x, shift, scale):
    return x * (1.0 + scale) + shift

def depthwise_conv(x, w, b):
    y = lax.conv_general_dilated(
        x, w[:, None, :].astype(x.dtype), window_strides=(1,), padding="SAME",
        dimension_numbers=("NWC", "WIO", "NWC"), feature_group_count=x.shape[-1])
    return y + b

def grid_positions(n_tokens):
    rows = n_tokens // GRID_W
    row_ids = jnp.repeat(jnp.arange(rows, dtype=jnp.float32), GRID_W)
    col_ids = jnp.tile(jnp.arange(GRID_W, dtype=jnp.float32), rows)
    return row_ids, col_ids

def rope_1d(x, pos):
    half = x.shape[-1] // 2
    inv_freq = ROPE_THETA ** (-jnp.arange(half, dtype=jnp.float32) / half)
    ang = pos[:, None] * inv_freq[None, :]
    cos = jnp.cos(ang)[None, :, None, :]
    sin = jnp.sin(ang)[None, :, None, :]
    x1 = x[..., :half].astype(jnp.float32)
    x2 = x[..., half:].astype(jnp.float32)
    return jnp.concatenate([x1 * cos - x2 * sin, x2 * cos + x1 * sin], axis=-1).astype(x.dtype)

def rope_2d(x, rows, cols):
    rd = x.shape[-1] // 2
    return jnp.concatenate([rope_1d(x[..., :rd], rows), rope_1d(x[..., rd:], cols)], axis=-1)

def diff_attend(q, k, v, lam):
    s = jnp.einsum("bqhpd,bkhpd->bhpqk", q, k).astype(jnp.float32) * (HEAD_DIM ** -0.5)
    p = jax.nn.softmax(s, axis=-1)
    a = p[:, :, 0] - lam * p[:, :, 1]
    return jnp.einsum("bhqk,bkhe->bqhe", a.astype(v.dtype), v)

def differential_attention(u_lat, u_ctx, w_qkv, w_out, lam_vec, subln_g, lam_init, with_ctx):
    bsz, n_lat, _ = u_lat.shape

    def project(u):
        n = u.shape[1]
        q, k, v = jnp.split(u @ w_qkv, 3, axis=-1)
        return (q.reshape(bsz, n, N_HEADS, 2, HEAD_DIM),
                k.reshape(bsz, n, N_HEADS, 2, HEAD_DIM),
                v.reshape(bsz, n, N_HEADS, V_HEAD_DIM))

    q_l, k_l, v_l = project(u_lat)
    q_c, k_c, v_c = project(u_ctx)
    rows, cols = grid_positions(n_lat)
    q_l = rope_2d(q_l.reshape(bsz, n_lat, 2 * N_HEADS, HEAD_DIM), rows, cols).reshape(q_l.shape)
    k_l = rope_2d(k_l.reshape(bsz, n_lat, 2 * N_HEADS, HEAD_DIM), rows, cols).reshape(k_l.shape)
    lf = lam_vec.astype(jnp.float32)
    lam = jnp.exp(jnp.sum(lf[0] * lf[1])) - jnp.exp(jnp.sum(lf[2] * lf[3])) + lam_init
    k_all = jnp.concatenate([k_c, k_l], axis=1)
    v_all = jnp.concatenate([v_c, v_l], axis=1)
    n_blk = n_lat // Q_BLOCK
    q_blocks = jnp.moveaxis(q_l.reshape(bsz, n_blk, Q_BLOCK, N_HEADS, 2, HEAD_DIM), 1, 0)
    o_l = lax.map(lambda qb: diff_attend(qb, k_all, v_all, lam), q_blocks)
    o_l = jnp.moveaxis(o_l, 0, 1).reshape(bsz, n_lat, N_HEADS, V_HEAD_DIM)

    def merge_heads(o):
        o = rms_norm_2(o, subln_g) * (1.0 - lam_init)
        return o.reshape(bsz, o.shape[1], D_MODEL) @ w_out

    y_l = merge_heads(o_l)
    y_c = merge_heads(diff_attend(q_c, k_c, v_c, lam)) if with_ctx else None
    return y_l, y_c

def hyena_filters(n, w1, b1, w2, b2, freq, w_out):
    bands = (HYENA_EMB_DIM - 1) // 2
    t = jnp.linspace(0.0, 1.0, n, dtype=jnp.float32)[:, None]
    w = 2.0 * math.pi * jnp.arange(n, dtype=jnp.float32)[:, None] / n
    f = jnp.linspace(1e-4, bands - 1, bands, dtype=jnp.float32)[None, :]
    z = jnp.concatenate([t, jnp.cos(f * w), -jnp.sin(f * w)], axis=-1)
    hdn = jnp.sin(freq * (z @ w1 + b1))
    for j in range(w2.shape[0]):
        hdn = jnp.sin(freq * (hdn @ w2[j] + b2[j]))
    h = (hdn @ w_out).reshape(n, 2, D_MODEL)
    deltas = jnp.abs(jnp.linspace(math.log(HYENA_DECAY_TARGET) / HYENA_SLOW_DECAY_PCT,
                                  math.log(HYENA_DECAY_TARGET) / HYENA_FAST_DECAY_PCT,
                                  D_MODEL, dtype=jnp.float32))
    h = h * jnp.exp(-t * deltas[None, :])[:, None, :]
    return h[:, 0], h[:, 1]

def two_sided_fft_conv(v, h_fwd, h_bwd):
    n = v.shape[1]
    kern = jnp.concatenate([h_fwd, jnp.zeros((1, h_fwd.shape[1]), h_fwd.dtype), h_bwd[:0:-1]], axis=0)
    vf = jnp.fft.rfft(v.astype(jnp.float32), n=2 * n, axis=1)
    kf = jnp.fft.rfft(kern.astype(jnp.float32), n=2 * n, axis=0)
    y = jnp.fft.irfft(vf * kf[None], n=2 * n, axis=1)[:, :n]
    return y.astype(v.dtype)

def hyena_mixer(u, w_in, b_in, w_short, b_short, fw1, fb1, fw2, fb2, ffreq, fw_out, d_bias, w_out, b_out):
    z = depthwise_conv(u @ w_in + b_in, w_short, b_short)
    x0, x1, v = jnp.split(z, 3, axis=-1)
    h_fwd, h_bwd = hyena_filters(u.shape[1], fw1, fb1, fw2, fb2, ffreq, fw_out)
    v = v * x1
    v = two_sided_fft_conv(v, h_fwd, h_bwd) + v * d_bias
    return (v * x0) @ w_out + b_out

def conformer_conv(u, w_pw1, b_pw1, w_dw, b_dw, ln_g, ln_b, w_pw2, b_pw2):
    a, g = jnp.split(u @ w_pw1 + b_pw1, 2, axis=-1)
    z = depthwise_conv(a * jax.nn.sigmoid(g), w_dw, b_dw)
    z = jax.nn.silu(layer_norm(z, ln_g, ln_b))
    return z @ w_pw2 + b_pw2

def squared_relu_mlp(u, w_in, w_out):
    return jnp.square(jax.nn.relu(u @ w_in)) @ w_out

def second_inputs(seed: int = 0) -> dict:
    key = jax.random.key(seed)
    ks = iter(jax.random.split(key, 48))
    D = D_MODEL

    def nrm(shape, scale):
        return scale * jax.random.normal(next(ks), shape, jnp.float32)

    return {
        "x": nrm((BATCH, SEQ, D), 1.0),
        "c": nrm((BATCH, D), 1.0),
        "ctx": nrm((BATCH, CTX_LEN, D), 1.0),
        "c_ctx": nrm((D,), 1.0),
        "w_mod": nrm((DEPTH, D, N_MOD * D), 0.5 * D ** -0.5),
        "b_mod": nrm((DEPTH, N_MOD * D), 0.02),
        "norm_mix_pre": 1.0 + nrm((DEPTH, D), 0.05),
        "norm_mix_post": 1.0 + nrm((DEPTH, D), 0.05),
        "norm_mlp_pre": 1.0 + nrm((DEPTH, D), 0.05),
        "norm_mlp_post": 1.0 + nrm((DEPTH, D), 0.05),
        "w_mlp_in": nrm((DEPTH, D, D_FF), D ** -0.5),
        "w_mlp_out": nrm((DEPTH, D_FF, D), D_FF ** -0.5),
        "attn_w_qkv": nrm((N_LAYERS_A, D, 3 * D), D ** -0.5),
        "attn_w_out": nrm((N_LAYERS_A, D, D), D ** -0.5),
        "attn_lambda": nrm((N_LAYERS_A, 4, HEAD_DIM), 0.1),
        "attn_subln": 1.0 + nrm((N_LAYERS_A, V_HEAD_DIM), 0.05),
        "hy_w_in": nrm((N_LAYERS_B, D, 3 * D), D ** -0.5),
        "hy_b_in": nrm((N_LAYERS_B, 3 * D), 0.02),
        "hy_w_short": nrm((N_LAYERS_B, HYENA_SHORT_WIDTH, 3 * D), HYENA_SHORT_WIDTH ** -0.5),
        "hy_b_short": nrm((N_LAYERS_B, 3 * D), 0.02),
        "hy_filt_w1": nrm((N_LAYERS_B, HYENA_EMB_DIM, HYENA_FILTER_ORDER), HYENA_EMB_DIM ** -0.5),
        "hy_filt_b1": nrm((N_LAYERS_B, HYENA_FILTER_ORDER), 0.1),
        "hy_filt_w2": nrm((N_LAYERS_B, 2, HYENA_FILTER_ORDER, HYENA_FILTER_ORDER), HYENA_FILTER_ORDER ** -0.5),
        "hy_filt_b2": nrm((N_LAYERS_B, 2, HYENA_FILTER_ORDER), 0.1),
        "hy_filt_freq": 1.0 + nrm((N_LAYERS_B, HYENA_FILTER_ORDER), 0.05),
        "hy_filt_w_out": nrm((N_LAYERS_B, HYENA_FILTER_ORDER, 2 * D), HYENA_FILTER_ORDER ** -0.5),
        "hy_bias": nrm((N_LAYERS_B, D), 1.0),
        "hy_w_out": nrm((N_LAYERS_B, D, D), D ** -0.5),
        "hy_b_out": nrm((N_LAYERS_B, D), 0.02),
        "cv_w_pw1": nrm((N_LAYERS_C, D, 2 * D), D ** -0.5),
        "cv_b_pw1": nrm((N_LAYERS_C, 2 * D), 0.02),
        "cv_w_dw": nrm((N_LAYERS_C, CONV_WIDTH, D), CONV_WIDTH ** -0.5),
        "cv_b_dw": nrm((N_LAYERS_C, D), 0.02),
        "cv_ln_g": 1.0 + nrm((N_LAYERS_C, D), 0.05),
        "cv_ln_b": nrm((N_LAYERS_C, D), 0.02),
        "cv_w_pw2": nrm((N_LAYERS_C, D, D), D ** -0.5),
        "cv_b_pw2": nrm((N_LAYERS_C, D), 0.02),
    }

def second_block(x, c, ctx, c_ctx, w_mod, b_mod, norm_mix_pre, norm_mix_post, norm_mlp_pre, norm_mlp_post,
              w_mlp_in, w_mlp_out, attn_w_qkv, attn_w_out, attn_lambda, attn_subln,
              hy_w_in, hy_b_in, hy_w_short, hy_b_short, hy_filt_w1, hy_filt_b1, hy_filt_w2, hy_filt_b2,
              hy_filt_freq, hy_filt_w_out, hy_bias, hy_w_out, hy_b_out,
              cv_w_pw1, cv_b_pw1, cv_w_dw, cv_b_dw, cv_ln_g, cv_ln_b, cv_w_pw2, cv_b_pw2):
    h_lat, h_ctx = x, ctx
    silu_c = jax.nn.silu(c)
    silu_cc = jax.nn.silu(c_ctx)
    for i in range(DEPTH):
        last = i == DEPTH - 1
        kind, j = i % N_MIXERS, i // N_MIXERS
        need_ctx_out = not last
        need_ctx_in = need_ctx_out or kind == 0
        mod_l = jnp.split((silu_c @ w_mod[i] + b_mod[i])[:, None, :], N_MOD, axis=-1)
        mod_c = jnp.split(silu_cc @ w_mod[i] + b_mod[i], N_MOD, axis=-1)
        u_l = modulate_2(rms_norm_2(h_lat, norm_mix_pre[i]), mod_l[0], mod_l[1])
        u_c = modulate_2(rms_norm_2(h_ctx, norm_mix_pre[i]), mod_c[0], mod_c[1]) if need_ctx_in else None
        if kind == 0:
            y_l, y_c = differential_attention(u_l, u_c, attn_w_qkv[j], attn_w_out[j], attn_lambda[j],
                                              attn_subln[j], 0.8 - 0.6 * math.exp(-0.3 * i), need_ctx_out)
        elif kind == 1:
            hp = (hy_w_in[j], hy_b_in[j], hy_w_short[j], hy_b_short[j], hy_filt_w1[j], hy_filt_b1[j],
                  hy_filt_w2[j], hy_filt_b2[j], hy_filt_freq[j], hy_filt_w_out[j], hy_bias[j],
                  hy_w_out[j], hy_b_out[j])
            y_l = hyena_mixer(u_l, *hp)
            y_c = hyena_mixer(u_c, *hp) if need_ctx_out else None
        else:
            cp = (cv_w_pw1[j], cv_b_pw1[j], cv_w_dw[j], cv_b_dw[j], cv_ln_g[j], cv_ln_b[j],
                  cv_w_pw2[j], cv_b_pw2[j])
            y_l = conformer_conv(u_l, *cp)
            y_c = conformer_conv(u_c, *cp) if need_ctx_out else None
        h_lat = h_lat + mod_l[2] * rms_norm_2(y_l, norm_mix_post[i])
        v_l = modulate_2(rms_norm_2(h_lat, norm_mlp_pre[i]), mod_l[3], mod_l[4])
        h_lat = h_lat + mod_l[5] * rms_norm_2(squared_relu_mlp(v_l, w_mlp_in[i], w_mlp_out[i]), norm_mlp_post[i])
        if need_ctx_out:
            h_ctx = h_ctx + mod_c[2] * rms_norm_2(y_c, norm_mix_post[i])
            v_c = modulate_2(rms_norm_2(h_ctx, norm_mlp_pre[i]), mod_c[3], mod_c[4])
            h_ctx = h_ctx + mod_c[5] * rms_norm_2(squared_relu_mlp(v_c, w_mlp_in[i], w_mlp_out[i]), norm_mlp_post[i])
    return h_lat


def setup_inputs(seed=0):
    out = dict(first_inputs(seed))
    for name, value in second_inputs(seed + 1).items():
        if name != "x":
            out[name + "_2"] = value
    return out


def reference(
    x, c, ctx, c_ctx, w_mod, b_mod, norm1_g, norm2_g, w_in, conv_w, w_out, lb_logits, peer_wq,
    peer_subkeys, peer_u, peer_v, final_g, c_2, ctx_2, c_ctx_2, w_mod_2, b_mod_2,
    norm_mix_pre_2, norm_mix_post_2, norm_mlp_pre_2, norm_mlp_post_2, w_mlp_in_2, w_mlp_out_2,
    attn_w_qkv_2, attn_w_out_2, attn_lambda_2, attn_subln_2, hy_w_in_2, hy_b_in_2, hy_w_short_2,
    hy_b_short_2, hy_filt_w1_2, hy_filt_b1_2, hy_filt_w2_2, hy_filt_b2_2, hy_filt_freq_2,
    hy_filt_w_out_2, hy_bias_2, hy_w_out_2, hy_b_out_2, cv_w_pw1_2, cv_b_pw1_2, cv_w_dw_2,
    cv_b_dw_2, cv_ln_g_2, cv_ln_b_2, cv_w_pw2_2, cv_b_pw2_2,
):
    x = first_block(
        x, c, ctx, c_ctx, w_mod, b_mod, norm1_g, norm2_g, w_in, conv_w, w_out, lb_logits,
        peer_wq, peer_subkeys, peer_u, peer_v, final_g,
    )
    return second_block(
        x, c_2, ctx_2, c_ctx_2, w_mod_2, b_mod_2, norm_mix_pre_2, norm_mix_post_2,
        norm_mlp_pre_2, norm_mlp_post_2, w_mlp_in_2, w_mlp_out_2, attn_w_qkv_2, attn_w_out_2,
        attn_lambda_2, attn_subln_2, hy_w_in_2, hy_b_in_2, hy_w_short_2, hy_b_short_2,
        hy_filt_w1_2, hy_filt_b1_2, hy_filt_w2_2, hy_filt_b2_2, hy_filt_freq_2, hy_filt_w_out_2,
        hy_bias_2, hy_w_out_2, hy_b_out_2, cv_w_pw1_2, cv_b_pw1_2, cv_w_dw_2, cv_b_dw_2,
        cv_ln_g_2, cv_ln_b_2, cv_w_pw2_2, cv_b_pw2_2,
    )


_drawn_inputs = setup_inputs


def setup_inputs(seed=0):
    import zlib

    import numpy as np

    out = dict(_drawn_inputs(seed))
    spreads = {}
    factors = {'ctx': 15.378,
     'c_ctx': 6.63,
     'norm_mlp_post_2': 2.872,
     'attn_lambda_2': 8.0,
     'attn_subln_2': 21.499,
     'hy_b_in_2': 4.31,
     'hy_b_short_2': 5.367,
     'hy_filt_freq_2': 3.697,
     'hy_b_out_2': 64.0,
     'norm_mix_pre_2': 2.779,
     'norm_mix_post_2': 2.839}
    for name, (base, spread) in spreads.items():
        noise = np.random.default_rng([zlib.crc32(name.encode()), seed]).standard_normal(out[name].shape)
        drawn = base * np.exp(spread * noise) if base else spread * noise
        out[name] = jnp.asarray(drawn.astype(out[name].dtype))
    for name, factor in factors.items():
        out[name] = (out[name] * factor).astype(out[name].dtype)
    return out
```

```python
from contextlib import ExitStack

import numpy as np

import concourse.bass as bass
from concourse import mybir
from concourse.alu_op_type import AluOpType as ALU

ACT = mybir.ActivationFunctionType
AX = mybir.AxisListType.X
F32 = mybir.dt.float32
U32 = mybir.dt.uint32

P = 128
T = 256
NT = T // P
D = 1024
KT = D // P
CW = 512
GRID_W = 64
HEADS = 4
HW = 512
LEVELS = 8
PH, PK, TOPK = 8, 128, 16
NSEL = PH * TOPK
NEXP = PK * PK
EPS = 1e-6
FLOOR = 1e-20
NEG = -3.0e38
AH, AD = 8, 64
LAM_INIT = 0.8 - 0.6
FF = 4096
EMB, ORDER = 33, 64
SLOTS = 8
GROUP = 4
TWO_PI = 2.0 * np.pi
ROUND = 1.5 * 2.0 ** 23


class Steps:

    def __init__(self, eng, sem):
        self.eng, self.sem, self.n = eng, sem, 0

    def do(self, ins):
        self.n += 1
        ins.then_inc(self.sem, 1)

    def settle(self):
        self.eng.wait_ge(self.sem, self.n)


class Linear:

    def __init__(self, src, n, g0, e0, gens):
        self.src, self.n, self.g0, self.e0, self.gens = src, n, g0, e0, gens


def program(nc, A, out):
    ctx = ExitStack()

    def sb(name, shape, dt=F32):
        return ctx.enter_context(nc.sbuf_tensor(name, shape, dt))

    def sem(name):
        return ctx.enter_context(nc.semaphore(name))

    with ctx:
        ring = sb("ring", [P, 2, KT, CW])
        xs = sb("xs", [P, NT, D])
        cs = sb("cs", [P, NT, D])
        hN = sb("hN", [P, NT, D])
        hT = sb("hT", [P, KT, T])
        vec = sb("vec", [P, 4, D])
        GAIN, SCALE, SHIFT, GATE = range(4)
        ident = sb("ident", [P, P])
        mean_mat = sb("mean_mat", [P, P])
        masks = sb("masks", [P, 14, P])
        iota16 = sb("iota16", [P, TOPK])
        subk = sb("subk", [P, 2 * PH, PK])
        states = sb("states", [P, 2, HEADS, P])
        lb = sb("lb", [P, 2, 2, HEADS])
        oml = sb("oml", [P, 2, 2, HEADS])
        convc = sb("convc", [P, 2, HEADS, 3])
        condS = sb("condS", [P, KT, 4])
        stat = sb("stat", [P, 16])
        eps = sb("eps", [P, 1])
        ARENA = 27392
        arena = sb("arena", [P, ARENA])
        ps = ctx.enter_context(nc.psum_tensor("ps", [P, 8, 512], F32))
        mods = nc.dram_tensor("mods", [4, 2, 6 * D], F32, kind="Internal").ap()

        class Area:

            def __init__(self):
                self.at = 0

            def take(self, *dims):
                n = int(np.prod(dims))
                flat = arena[:, self.at:self.at + n]
                self.at += n
                assert self.at <= ARENA, self.at
                if len(dims) == 1:
                    return flat
                names = "abcd"[:len(dims)]
                return flat.rearrange(f"p ({' '.join(names)}) -> p {' '.join(names)}",
                                      **{k: v for k, v in zip(names, dims)})

        ring_full = [sem(f"ring_full{s}") for s in range(2)]
        ring_done = sem("ring_done")
        bank_free = sem("bank_free")
        consts_in = sem("consts_in")
        cond_ready = sem("cond_ready")
        mod_rows = sem("mod_rows")
        mod_stored = sem("mod_stored")
        vec_full = sem("vec_full")
        vec_used = sem("vec_used")
        normed = sem("normed")
        tr_done = sem("tr_done")
        tr_out = sem("tr_out")
        lev_ready = sem("lev_ready")
        lev_mm = sem("lev_mm")
        scan_ready = sem("scan_ready")
        o_done = sem("o_done")
        o_sq = sem("o_sq")
        o_ms = sem("o_ms")
        o_root = sem("o_root")
        kr_turned = sem("kr_turned")
        kr_out = sem("kr_out")
        st_done = sem("st_done")
        st_out = sem("st_out")
        mix_ready = sem("mix_ready")
        resid = sem("resid")
        subk_in = sem("subk_in")
        score_mm = sem("score_mm")
        score_out = sem("score_out")
        gate_sub = sem("gate_sub")
        gate_exp = sem("gate_exp")
        picks = sem("picks")
        idx_ready = sem("idx_ready")
        gathers_sent = sem("gathers_sent")
        u_full = [sem(f"u_full{s}") for s in range(SLOTS)]
        v_full = [sem(f"v_full{s}") for s in range(SLOTS)]
        dots_ready = sem("dots_ready")
        gelu_done = sem("gelu_done")
        coef_ready = sem("coef_ready")
        axpy_done = sem("axpy_done")
        ctx2_in = sem("ctx2_in")
        tab_in = sem("tab_in")
        lam_sums = sem("lam_sums")
        lam_exps = sem("lam_exps")
        heads_in = sem("heads_in")
        s_mm = sem("s_mm")
        s_bias = sem("s_bias")
        s_exp = sem("s_exp")
        a_ready = sem("a_ready")
        a_turned = sem("a_turned")
        a_out = sem("a_out")
        ao_mm = sem("ao_mm")
        ao_sq = sem("ao_sq")
        ao_norm = sem("ao_norm")
        y_out = sem("y_out")
        hid = sem("hid")
        f_mm = sem("f_mm")
        f_arg = sem("f_arg")
        f_lin = sem("f_lin")
        f_red = sem("f_red")
        f_sin = sem("f_sin")
        f_h = sem("f_h")
        f_taps = sem("f_taps")
        f_pm = sem("f_pm")
        k_mm = sem("k_mm")
        k_out = sem("k_out")
        vv_ready = sem("vv_ready")
        y_freq = sem("y_freq")
        conv_mm = sem("conv_mm")
        stored = sem("stored")
        wall = sem("wall")
        ms_ready = sem("ms_ready")
        root_ready = sem("root_ready")
        dve_step, act_step, pool_step = sem("dve_step"), sem("act_step"), sem("pool_step")

        plan = []
        place = [0, 0]

        def linear(src, n, gens=None):
            L = Linear(src, n, place[0], place[1], gens or n)
            place[0] += n
            place[1] += L.gens
            plan.append(L)
            return L

        def chunked(w, c0=0):
            v = w.rearrange("(k p) n -> p k n", p=P)
            return lambda c: v[:, :, bass.ds(c * CW + c0 * CW, CW)]

        def chunked_deep(w):
            v = w.rearrange("(g k p) n -> g p k n", k=KT, p=P)
            return lambda c: v[c % 4, :, :, (c // 4) * CW:(c // 4 + 1) * CW]

        L_mod = [linear(chunked(A["w_mod4"][l]), 12) for l in range(4)]
        L_in, L_out, L_wq = {}, {}, {}

        def plan_in(m, l, n):
            L_in[m] = linear(chunked(A["w_in"][l]), n)

        def plan_out(m, l):
            L_out[m] = linear(chunked(A["w_out"][l]), 2)

        def plan_wq(p, l):
            L_wq[p] = linear(chunked(A["peer_wq"][l]), 4)

        plan_in(0, 0, 8), plan_out(0, 0), plan_in(1, 0, 8), plan_out(1, 0)
        plan_wq(0, 0), plan_wq(1, 0)
        plan_in(2, 1, 3), plan_in(3, 1, 8), plan_out(3, 1), plan_wq(2, 1)
        L_kv = linear(chunked(A["attn_w_qkv"], 2), 4)
        L_qkv = linear(chunked(A["attn_w_qkv"]), 6)
        L_ao = linear(chunked(A["attn_w_out"]), 2)
        L_up, L_down = {}, {}
        L_up[0] = linear(chunked(A["w_mlp_in"][0]), 8)
        L_down[0] = linear(chunked_deep(A["w_mlp_out"][0]), 8, 2)
        L_hin = linear(chunked(A["hy_w_in"]), 6)
        L_hout = linear(chunked(A["hy_w_out"]), 2)
        L_up[1] = linear(chunked(A["w_mlp_in"][1]), 8)
        L_down[1] = linear(chunked_deep(A["w_mlp_out"][1]), 8, 2)

        def mod(l, who, j):
            return mods[l, who, j * D:(j + 1) * D]

        def pre(l, who, g, j):
            return [(GAIN, g), (SHIFT, mod(l, who, j)), (SCALE, mod(l, who, j + 1))]

        X, C = 0, 1
        rows = {}
        rows["n_c0"] = pre(0, C, A["norm1_g"][0], 0)
        rows["r_c0"] = [(GATE, mod(0, C, 2))]
        rows["n_x0"] = pre(0, X, A["norm1_g"][0], 0)
        rows["r_x0"] = [(GATE, mod(0, X, 2))]
        rows["p_c0"] = pre(0, C, A["norm2_g"][0], 3)
        rows["q_c0"] = [(GATE, mod(0, C, 5))]
        rows["p_x0"] = pre(0, X, A["norm2_g"][0], 3)
        rows["q_x0"] = [(GATE, mod(0, X, 5))]
        rows["n_c1"] = pre(1, C, A["norm1_g"][1], 0)
        rows["n_x1"] = pre(1, X, A["norm1_g"][1], 0)
        rows["r_x1"] = [(GATE, mod(1, X, 2))]
        rows["p_x1"] = pre(1, X, A["norm2_g"][1], 3)
        rows["q_x1"] = [(GATE, mod(1, X, 5))]
        rows["final"] = [(GAIN, A["final_g"])]
        rows["n_kv"] = pre(2, C, A["norm_mix_pre"][0], 0)
        rows["n_q"] = pre(2, X, A["norm_mix_pre"][0], 0)
        rows["o_0"] = [(GAIN, A["norm_mix_post"][0]), (GATE, mod(2, X, 2))]
        rows["n_m0"] = pre(2, X, A["norm_mlp_pre"][0], 3)
        rows["m_0"] = [(GAIN, A["norm_mlp_post"][0]), (GATE, mod(2, X, 5))]
        rows["n_h"] = pre(3, X, A["norm_mix_pre"][1], 0)
        rows["o_1"] = [(GAIN, A["norm_mix_post"][1]), (GATE, mod(3, X, 2)), (SHIFT, A["hy_b_out"])]
        rows["n_m1"] = pre(3, X, A["norm_mlp_pre"][1], 3)
        rows["m_1"] = [(GAIN, A["norm_mlp_post"][1]), (GATE, mod(3, X, 5))]
        stage_no, rows_in, total = {}, {}, 0
        for j, (name, rs) in enumerate(rows.items()):
            stage_no[name] = j
            total += 16 * len(rs)
            rows_in[name] = total
        norm_order = [s for s in rows if s[0] in "np" and s != "final"]
        norm_no = {s: j for j, s in enumerate(norm_order)}

        turn_no = {s: j for j, s in enumerate(
            ["n_c0", "n_x0", "p_c0", "p_x0", "n_c1", "n_x1", "p_x1", "n_kv", "n_q", "q", "kc", "kx", "ao",
             "n_m0", "n_h", "vv", "n_m1"])}

        resid_no = {s: j for j, s in enumerate(
            ["r_c0", "r_x0", "q_c0", "q_x0", "r_x1", "q_x1", "final", "o_0", "m_0", "o_1", "m_1"])}

        a = Area()
        mod_row = a.take(4, 6 * D)

        a = Area()
        SF, KF, SB, KB, Q, G, CG, BG, HV = [a.take(HEADS, T) for _ in range(9)]
        QF, QB = a.take(HEADS, T), a.take(HEADS, T)
        tots = [[a.take(HEADS * T >> l) for l in range(1, LEVELS + 1)] for _ in range(2)]
        att = a.take(NT, HEADS, T)
        ivN = a.take(NT, HW)
        KS, OSQ, ORS, CU = [a.take(HEADS, T) for _ in range(4)]
        mixT = a.take(KT, T)
        KRN = a.take(2, NT, HEADS, P)

        a = Area()
        eidx_f = a.take(NT, NSEL)
        gates = a.take(NT, NSEL)
        eidx = a.take(NT, NSEL).bitcast(U32)
        kept = a.at
        qrT = a.take(2 * PH, T)
        sc = a.take(NT, 2 * PH, PK)
        wk = a.take(2 * PH, PK)
        vals = a.take(PH, 2, TOPK)
        vidx = a.take(PH, 2, TOPK).bitcast(U32)
        vidx_f = a.take(PH, 2, TOPK)
        cand = a.take(PH, TOPK, TOPK)
        cwk = a.take(PH, TOPK * TOPK)
        top = a.take(NT, PH, TOPK)
        pos = a.take(PH, TOPK).bitcast(U32)
        pos2 = a.take(2, NSEL).bitcast(U32)
        pos_f = a.take(2, NSEL)
        eqs = a.take(NSEL, TOPK)
        sel = a.take(2, NSEL)
        zsum = a.take(NT, PH)

        a = Area()
        a.at = kept
        ubuf = a.take(SLOTS, D)
        vbuf = a.take(SLOTS, D)
        acc = a.take(2, D)
        dots = a.take(SLOTS)
        coef = a.take(SLOTS)
        idx_col = a.take(SLOTS).bitcast(U32)

        a = Area()
        qN, kcN, kxN = a.take(NT, D), a.take(NT, D), a.take(NT, D)
        vN = a.take(2 * NT, D)
        qT = a.take(AH, T)
        kT = a.take(AH, 2 * T)
        prob = a.take(2, 2, 2 * T)
        aT = a.take(2, 4, P)
        oN = a.take(NT, D)
        rope_tmp = a.take(D)
        cosT, sinT = a.take(NT, AD), a.take(NT, 2, 2, 16)
        subln = a.take(P)
        lam_in = a.take(4, AD)
        lam_tmp = a.take(2, AD)
        a_small = a.take(2, 8)
        yA = oN

        a = Area()
        hidT = a.take(FF // P, T)
        yM = a.take(NT, D)

        a = Area()
        zT = a.take(24, T)
        zc = a.take(24, T)
        Kf = a.take(2, NT, D)
        Vf = a.take(2, NT, D)
        vNat = a.take(NT, D)
        dft = a.take(2, NT, T)
        idft = a.take(2, NT, T)
        hyb = a.take(24)
        hysw = a.take(24, 3)
        hysb = a.take(24)
        hyd = a.take(KT)
        taps = zT.rearrange("p a b -> p (a b)")[:, 0:NT * 2 * D].rearrange("p (t d) -> p t d", t=NT)
        decay = zc.rearrange("p a b -> p (a b)")[:, 0:NT * D].rearrange("p (t d) -> p t d", t=NT)
        f_out = zc.rearrange("p a b -> p (a b)")[:, NT * D:2 * NT * D]
        zrest = zc.rearrange("p a b -> p (a b)")[:, 2 * NT * D:3 * NT * D]
        f_emb, f_hid = zrest[:, 0:T], zrest[:, T:2 * T]
        f_x, f_n = zrest[:, 2 * T:3 * T], zrest[:, 3 * T:4 * T]
        f_w = zrest[:, 4 * T:4 * T + 3 * ORDER].rearrange("p (j o) -> p j o", j=3)
        f_b = zrest[:, 5 * T:5 * T + 8]
        Yf = zT.rearrange("p a b -> p (a b)")[:, 0:2 * NT * D].rearrange("p (c t d) -> p c t d", c=2, t=NT)
        ytmp = zT.rearrange("p a b -> p (a b)")[:, 2 * NT * D:3 * NT * D].rearrange("p (t d) -> p t d", t=NT)
        yH = Vf[:, 0]

        consts = [
            (ident[:, :], A["ident"]), (mean_mat[:, :], A["mean_mat"]), (masks[:, :, :], A["masks"]),
            (eps[:, :], A["eps"]), (iota16[:, :], A["iota16"]), (lb[:, :, :, :], A["lbT"]), (convc[:, :, :, :], A["convT"]),
            (condS[:, :, :], A["condT"]), (xs[:, :, :], A["x"].rearrange("(t p) d -> p t d", p=P)),
            (cs[:, :, :], A["ctx"].rearrange("(t p) d -> p t d", p=P)),
            (mod_row[0:1], A["b_mod4"].unsqueeze(0)), (mod_row[1:2], A["b_mod4"].unsqueeze(0)),
        ]
        N_CONSTS = len(consts)
        att_tabs = [
            (cosT, A["rope_cos"].rearrange("(t p) d -> p t d", p=P)),
            (sinT.rearrange("p t c x f -> p t (c x f)"), A["rope_sin"].rearrange("(t p) d -> p t d", p=P)),
            (subln, A["attn_subln"].partition_broadcast(P)),
            (lam_in.rearrange("p a d -> p (a d)"), A["attn_lambda"].partition_broadcast(P)),
        ]
        N_ATT_TABS = len(att_tabs)
        hy_tabs = [
            (dft, A["dft"].rearrange("c (t p) f -> p c t f", p=P)),
            (idft, A["idft"].rearrange("c (t p) f -> p c t f", p=P)),
            (decay, A["decay"].rearrange("(t p) d -> p t d", p=P)),
            (f_out[0:ORDER, :], A["hy_filt_w_out"]), (f_emb[0:EMB, :], A["filt_emb"]),
            (f_w[0:EMB, 0, :], A["hy_filt_w1"]), (f_w[0:ORDER, 1:3, :], A["hy_filt_w2"].rearrange("j i o -> i j o")),
            (f_b[0:ORDER, 0:4], A["filt_b"]),
            (hyb, A["hy_bT"]), (hysw, A["hy_swT"]), (hysb, A["hy_sbT"]), (hyd, A["hy_dT"]),
        ]
        N_HY_TABS = len(hy_tabs)

        block = ctx.enter_context(nc.Block())

        def wall_at(eng, n):
            eng.drain().then_inc(wall, 1)
            eng.wait_ge(wall, 4 * (n + 1))

        @block.sync
        def _(sp):
            def chunk(L, c, i, u):
                g = L.g0 + u
                sp.wait_ge(ring_done, i * 2 + (g + 1))
                sp.dma_start(ring[:, g % 2], L.src(c)).then_inc(ring_full[g % 2], 16)

            for L in plan:
                if L.gens == L.n and L.n >= 4:
                    with sp.Fori(0, L.n // 2) as i:
                        for u in range(2):
                            chunk(L, i * 2 + u, i, u)
                else:
                    for c in range(L.n):
                        chunk(L, c, 0, c)

        @block.tensor
        def _(pe):
            pe.sem_inc(ring_done, 2)
            pe.wait_ge(consts_in, 16 * N_CONSTS)

            def enter(L, u, i=0, e=None):
                g = L.g0 + u
                pe.wait_ge(ring_full[g % 2], i * 16 + 16 * (g // 2 + 1))
                if e is not None:
                    pe.wait_ge(bank_free, i * 2 + (e + 1))
                return g % 2

            def tokens_chunk(s, e, lhs, k0=0, first=True, last=True):
                for t in range(NT):
                    for k in range(KT):
                        mm = pe.matmul(ps[:, 2 * (e % 2) + t, :], lhs[:, k0 + k, t * P:(t + 1) * P],
                                       ring[:, s, k, :], start=first and k == 0, stop=last and k == KT - 1)
                mm.then_inc(ring_done, 1)

            def features_chunk(s, e, rhs):
                for b in range(4):
                    o = ps[:, 2 * (e % 2) + b // 2, (b % 2) * T:(b % 2 + 1) * T]
                    for k in range(KT):
                        mm = pe.matmul(o, ring[:, s, k, b * P:(b + 1) * P], rhs[:, k, :],
                                       start=k == 0, stop=k == KT - 1)
                mm.then_inc(ring_done, 1)

            def features(L, rhs, c0=0):
                if L.n - c0 >= 4 and (L.n - c0) % 2 == 0:
                    with pe.Fori(0, (L.n - c0) // 2) as i:
                        for u in range(2):
                            features_chunk(enter(L, c0 + u, i, L.e0 + c0 + u), L.e0 + c0 + u, rhs)
                else:
                    for c in range(c0, L.n):
                        features_chunk(enter(L, c, 0, L.e0 + c), L.e0 + c, rhs)

            def tokens(L, lhs):
                if L.n >= 4:
                    with pe.Fori(0, L.n // 2) as i:
                        for u in range(2):
                            tokens_chunk(enter(L, u, i, L.e0 + u), L.e0 + u, lhs)
                else:
                    for c in range(L.n):
                        tokens_chunk(enter(L, c, 0, L.e0 + c), L.e0 + c, lhs)

            def turn(name, src, ready, value):
                r = turn_no[name]
                for t in range(NT):
                    pe.wait_ge(ready, value(t))
                    if r:
                        pe.wait_ge(tr_out, 4 * r)
                    for half in range(2):
                        for j in range(4):
                            k = 4 * half + j
                            mm = pe.transpose(ps[:, 4 + 2 * t + half, j * P:(j + 1) * P],
                                              src[:, t, k * P:(k + 1) * P], ident[:, :])
                        mm.then_inc(tr_done, 1)

            def turn_norm(name):
                turn(name, hN, normed, lambda t: NT * norm_no[name] + t + 1)
                pe.wait_ge(tr_out, 4 * (turn_no[name] + 1))

            def mixer(m):
                L = L_in[m]
                tokens_chunk(enter(L, 0, 0, L.e0), L.e0, hT)
                if m == 2:
                    features(L, hT, 1)
                else:
                    features_chunk(enter(L, 1, 0, L.e0 + 1), L.e0 + 1, hT)
                    features(L, hT, 2)
                n = {0: 0, 1: 1, 3: 2}.get(m)
                if m != 2:
                    for j in range(9):
                        pe.wait_ge(lev_ready, 9 * n + j + 1)
                        for h in range(HEADS):
                            cols = slice(h * P, (h + 1) * P)
                            if j == 0:
                                for t in range(NT):
                                    ts = slice(t * P, (t + 1) * P)
                                    mm = pe.matmul(ps[:, 4 + t, cols], KS[:, h, ts], Q[:, h, ts], start=True, stop=True)
                            elif j < 8:
                                for t in range(NT):
                                    ts = slice(t * P, (t + 1) * P)
                                    pe.matmul(ps[:, 4 + t, cols], KF[:, h, ts], QF[:, h, ts], start=True, stop=True)
                                    mm = pe.matmul(ps[:, 6 + t, cols], KB[:, h, ts], QB[:, h, ts], start=True, stop=True)
                            else:
                                pe.matmul(ps[:, 4, cols], KF[:, h, 0:P], QF[:, h, P:T], start=True, stop=True)
                                mm = pe.matmul(ps[:, 5, cols], KB[:, h, P:T], QB[:, h, 0:P], start=True, stop=True)
                        mm.then_inc(lev_mm, 1)
                pe.wait_ge(scan_ready, m + 1)
                if m != 2:
                    for h in range(HEADS):
                        o = ps[:, 4 + h // 2, (h % 2) * T:(h % 2 + 1) * T]
                        for st in range(NT):
                            mm = pe.matmul(o, ivN[:, st, h * P:(h + 1) * P], att[:, st, h, :], start=st == 0,
                                           stop=m == 0 and st == NT - 1)
                        if m != 0:
                            if h == 0:
                                pe.wait_ge(st_out, 1 if m == 1 else 2)
                            pe.matmul(o, states[:, 0, h, :], QF[:, h, :], start=False, stop=False)
                            mm = pe.matmul(o, states[:, 1, h, :], QB[:, h, :], start=False, stop=True)
                    mm.then_inc(o_done, 1)
                    pe.wait_ge(o_sq, n + 1)
                    osq = OSQ.rearrange("p h t -> p (h t)")
                    for j in range(2):
                        mm = pe.matmul(ps[:, 6 + j, :], mean_mat[:, :], osq[:, j * 512:(j + 1) * 512], start=True, stop=True)
                    mm.then_inc(o_ms, 1)
                if m in (0, 2):
                    if m == 0:
                        pe.wait_ge(mix_ready, 1)
                    k = m // 2
                    for d, src in enumerate((KF, KB)):
                        for st in range(NT):
                            for h in range(HEADS):
                                mm = pe.transpose(ps[:, 4 + 2 * d + st, h * P:(h + 1) * P],
                                                  src[:, h, st * P:(st + 1) * P], ident[:, :])
                    mm.then_inc(kr_turned, 1)
                    pe.wait_ge(kr_out, k + 1)
                    for d in range(2):
                        for h in range(HEADS):
                            for st in range(NT):
                                mm = pe.matmul(ps[:, 4 + d, h * P:(h + 1) * P], KRN[:, d, st, h, :],
                                               ivN[:, st, h * P:(h + 1) * P], start=st == 0, stop=st == NT - 1)
                    mm.then_inc(st_done, 1)
                if m != 2:
                    pe.wait_ge(mix_ready, n + 1)
                    tokens(L_out[m], mixT)

            def peer(p):
                features(L_wq[p], hT)
                pe.wait_ge(bank_free, L_wq[p].e0 + 4 + 2)
                pe.wait_ge(subk_in, 16 * (p + 1))
                for t in range(NT):
                    if t:
                        pe.wait_ge(score_out, NT * p + t)
                    for j in range(2 * PH):
                        mm = pe.matmul(ps[:, 4 + j // 4, (j % 4) * P:(j % 4 + 1) * P], qrT[:, j, t * P:(t + 1) * P],
                                       subk[:, j, :], start=True, stop=True)
                    mm.then_inc(score_mm, 1)

            def attention():
                for j in range(NT * AH):
                    h, t = j // NT, j % NT
                    b, par = 4 + 2 * (j % 2), j % 2
                    if j >= 2:
                        pe.wait_ge(s_exp, 2 * (j - 1))
                    for half in range(2):
                        ds_ = slice(half * AD, (half + 1) * AD)
                        mm = pe.matmul(ps[:, b + half, :], qT[ds_, h, t * P:(t + 1) * P], kT[ds_, h, :], start=True, stop=True)
                    mm.then_inc(s_mm, 1)
                    if j >= 1:
                        attention_out(j - 1)
                attention_out(NT * AH - 1)

            def attention_out(j):
                h, par = j // NT, j % 2
                pe.wait_ge(a_ready, j + 1)
                for kt in range(4):
                    mm = pe.transpose(ps[:, par, kt * P:(kt + 1) * P], prob[:, par, 0, kt * P:(kt + 1) * P], ident[:, :])
                mm.then_inc(a_turned, 1)
                pe.wait_ge(a_out, j + 1)
                if j >= 2:
                    pe.wait_ge(ao_norm, j - 1)
                for kt in range(4):
                    mm = pe.matmul(ps[:, 2 + par, 0:P], aT[:, par, kt, :], vN[:, kt, h * P:(h + 1) * P],
                                   start=kt == 0, stop=kt == 3)
                mm.then_inc(ao_mm, 1)

            def mlp(i):
                turn_norm(f"n_m{i}")
                features(L_up[i], hT)
                L = L_down[i]
                for c in range(8):
                    e = L.e0 + c // 4
                    s = enter(L, c, 0, e if c % 4 == 0 else None)
                    pe.wait_ge(hid, 8 * i + min(2 * (c % 4) + 2, 8))
                    tokens_chunk(s, e, hidT, KT * (c % 4), c % 4 == 0, c % 4 == 3)

            pe.wait_ge(cond_ready, 1)
            for l in range(4):
                L = L_mod[l]
                with pe.Fori(0, L.n // 2) as i:
                    for u in range(2):
                        s = enter(L, u, i, L.e0 + u)
                        for k in range(KT):
                            mm = pe.matmul(ps[0:2, 2 * ((L.e0 + u) % 2), :], condS[:, k, 2 * (l // 2):2 * (l // 2) + 2],
                                           ring[:, s, k, :], start=k == 0, stop=k == KT - 1)
                        mm.then_inc(ring_done, 1)
            wall_at(pe, 0)
            for m, name in ((0, "n_c0"), (1, "n_x0")):
                turn_norm(name)
                mixer(m)
                wall_at(pe, 1 + m)
            for p, name in ((0, "p_c0"), (1, "p_x0")):
                turn_norm(name)
                peer(p)
                wall_at(pe, 3 + 2 * p)
                wall_at(pe, 4 + 2 * p)
            turn_norm("n_c1")
            mixer(2)
            wall_at(pe, 7)
            turn_norm("n_x1")
            mixer(3)
            wall_at(pe, 8)
            turn_norm("p_x1")
            peer(2)
            wall_at(pe, 9)
            wall_at(pe, 10)
            turn_norm("n_kv")
            tokens(L_kv, hT)
            turn_norm("n_q")
            tokens(L_qkv, hT)
            turn("q", qN, heads_in, lambda t: t + 1)
            turn("kc", kcN, bank_free, lambda t: L_kv.e0 + 2 + 2)
            turn("kx", kxN, heads_in, lambda t: NT + t + 1)
            pe.wait_ge(tr_out, 4 * (turn_no["kx"] + 1))
            attention()
            turn("ao", oN, ao_norm, lambda t: NT * AH)
            pe.wait_ge(tr_out, 4 * (turn_no["ao"] + 1))
            tokens(L_ao, hT)
            wall_at(pe, 11)
            mlp(0)
            wall_at(pe, 12)
            pe.wait_ge(tab_in, 16 * (N_ATT_TABS + N_HY_TABS))
            for j in range(3):
                if j:
                    pe.wait_ge(f_sin, j)
                n_in = EMB if j == 0 else ORDER
                pe.matmul(ps[0:ORDER, 4, 0:T], f_w[0:n_in, j, :], (f_emb if j == 0 else f_hid)[0:n_in, :],
                          start=True, stop=True).then_inc(f_mm, 1)
            pe.wait_ge(f_sin, 3)
            for t in range(NT):
                if t:
                    pe.wait_ge(f_taps, 1)
                for c in range(4):
                    mm = pe.matmul(ps[:, 4 + c, :], f_hid[0:ORDER, t * P:(t + 1) * P], f_out[0:ORDER, c * 512:(c + 1) * 512],
                                   start=True, stop=True)
                mm.then_inc(f_h, 1)

            def spectrum(srcs, n):
                for part in range(2):
                    if n or part:
                        pe.wait_ge(k_out, 2 * n + part)
                    for ft in range(NT):
                        for c in range(2):
                            for tt in range(NT):
                                mm = pe.matmul(ps[:, 4 + 2 * ft + c, :], dft[:, part, tt, ft * P:(ft + 1) * P],
                                               srcs[part](tt, c), start=tt == 0, stop=tt == NT - 1)
                    mm.then_inc(k_mm, 1)

            pe.wait_ge(f_pm, 1)
            spectrum([lambda tt, c: taps[:, tt, c * 512:(c + 1) * 512],
                      lambda tt, c: taps[:, tt, D + c * 512:D + (c + 1) * 512]], 0)
            wall_at(pe, 13)
            turn_norm("n_h")
            features(L_hin, hT)
            r = turn_no["vv"]
            pe.wait_ge(vv_ready, 1)
            for t in range(NT):
                for half in range(2):
                    for j in range(4):
                        mm = pe.transpose(ps[:, 4 + 2 * t + half, j * P:(j + 1) * P],
                                          zc[:, 16 + 4 * half + j, t * P:(t + 1) * P], ident[:, :])
                    mm.then_inc(tr_done, 1)
            pe.wait_ge(tr_out, 4 * (r + 1))
            spectrum([lambda tt, c: vNat[:, tt, c * 512:(c + 1) * 512]] * 2, 1)
            pe.wait_ge(y_freq, 1)
            for b in range(KT):
                o = ps[:, 4 + b // 2, (b % 2) * T:(b % 2 + 1) * T]
                for part in range(2):
                    for ft in range(NT):
                        mm = pe.matmul(o, Yf[:, part, ft, b * P:(b + 1) * P], idft[:, part, ft, :],
                                       start=part == 0 and ft == 0, stop=part == 1 and ft == NT - 1)
            mm.then_inc(conv_mm, 1)
            pe.wait_ge(vv_ready, 2)
            tokens(L_hout, hT)
            wall_at(pe, 14)
            mlp(1)
            wall_at(pe, 15)

        @block.scalar
        def _(act):
            st = Steps(act, act_step)
            roots = [0]

            def root(col):
                roots[0] += 1
                act.wait_ge(ms_ready, roots[0])
                act.activation(stat[:, col:col + NT], stat[:, col:col + NT], ACT.Sqrt, bias=eps[:, 0:1]).then_inc(root_ready, 1)

            def turn_norm(name):
                root(0)
                turn(name, hT)
            act.sem_inc(bank_free, 2)
            act.wait_ge(consts_in, 16 * N_CONSTS)
            act.activation(condS[:, :, :], condS[:, :, :], ACT.Silu).then_inc(cond_ready, 1)

            def pair(e):
                return ps[:, 2 * (e % 2):2 * (e % 2) + 2, :].rearrange("p a b -> p (a b)")

            def chunk_there(L, c):
                act.wait_ge(ring_done, L.g0 + c + 3)

            def copy_features(L, c, dst, func=ACT.Copy):
                chunk_there(L, c)
                act.activation(dst.rearrange("p b t -> p (b t)"), pair(L.e0 + c), func).then_inc(bank_free, 1)

            def copy_tokens(L, c, dst):
                chunk_there(L, c)
                e = L.e0 + c
                act.activation(dst, ps[:, 2 * (e % 2):2 * (e % 2) + 2, :], ACT.Copy).then_inc(bank_free, 1)

            def turn(name, dst):
                r = turn_no[name]
                for q in range(4):
                    t, half = q // 2, q % 2
                    act.wait_ge(tr_done, 4 * r + q + 1)
                    act.activation(dst[:, 4 * half:4 * half + 4, t * P:(t + 1) * P],
                                   ps[:, 4 + q, :].rearrange("p (j t) -> p j t", j=4), ACT.Copy).then_inc(tr_out, 1)

            def mixer(m):
                L = L_in[m]
                copy_tokens(L, 0, ivN)
                for c, s, k in ((1, SF, KF), (2, SB, KB)):
                    chunk_there(L, c)
                    act.activation(s.rearrange("p h t -> p (h t)"), pair(L.e0 + c), ACT.Sigmoid)
                    act.activation(k.rearrange("p h t -> p (h t)"), pair(L.e0 + c), ACT.Sigmoid,
                                   scale=-1.0).then_inc(bank_free, 1)
                if m != 2:
                    n = {0: 0, 1: 1, 3: 2}[m]
                    copy_features(L, 3, Q)
                    copy_features(L, 4, G, ACT.Silu)
                    for c, dst in ((5, CG), (6, BG), (7, HV)):
                        copy_features(L, c, dst)
                    act.wait_ge(o_done, n + 1)
                    act.activation(OSQ.rearrange("p h t -> p (h t)"), ps[:, 4:6, :].rearrange("p a b -> p (a b)"),
                                   ACT.Square).then_inc(o_sq, 1)
                    act.wait_ge(o_ms, n + 1)
                    act.activation(ORS.rearrange("p h t -> p (h t)"), ps[:, 6:8, :].rearrange("p a b -> p (a b)"),
                                   ACT.Sqrt, bias=eps[:, 0:1]).then_inc(o_root, 1)
                if m in (0, 2):
                    k = m // 2
                    act.wait_ge(kr_turned, k + 1)
                    act.activation(KRN.rearrange("p d s h k -> p (d s) (h k)"), ps[:, 4:8, :], ACT.Copy).then_inc(kr_out, 1)
                    act.wait_ge(st_done, k + 1)
                    act.activation(states[:, :, :, :].rearrange("p d h v -> p d (h v)"), ps[:, 4:6, :],
                                   ACT.Copy).then_inc(st_out, 1)

            def peer(p):
                for c in range(4):
                    copy_features(L_wq[p], c, qrT[:, 4 * c:4 * c + 4, :])
                for t in range(NT):
                    act.wait_ge(score_mm, NT * p + t + 1)
                    act.activation(sc[:, t].rearrange("p j k -> p (j k)"), ps[:, 4:8, :].rearrange("p a b -> p (a b)"),
                                   ACT.Copy).then_inc(score_out, 1)
                act.wait_ge(gate_sub, p + 1)
                act.activation(top, top, ACT.Exp).then_inc(gate_exp, 1)

            def peer_gelu(p):
                for t in range(NT):
                    K = (NT * p + t) * (NSEL // GROUP)
                    with act.Fori(0, NSEL // SLOTS) as i:
                        for half in range(SLOTS // GROUP):
                            s = slice(half * GROUP, (half + 1) * GROUP)
                            act.wait_ge(dots_ready, i * 2 + (K + half + 1))
                            act.activation(coef[:, s], dots[:, s], ACT.Gelu).then_inc(gelu_done, 1)

            def attention():
                for j in range(NT * AH):
                    b, par = 4 + 2 * (j % 2), j % 2
                    act.wait_ge(s_bias, j + 1)
                    if j >= 2:
                        act.wait_ge(a_turned, j - 1)
                    for half in range(2):
                        act.activation(prob[:, par, half, :], ps[:, b + half, :], ACT.Exp, scale=AD ** -0.5,
                                       bias=a_small[:, par, half:half + 1],
                                       accum_out=a_small[:, par, 2 + half:3 + half]).then_inc(s_exp, 1)
                    if j >= 1:
                        attention_out(j - 1)
                attention_out(NT * AH - 1)

            def attention_out(j):
                par = j % 2
                act.wait_ge(a_turned, j + 1)
                if j >= 2:
                    act.wait_ge(ao_mm, j - 1)
                act.activation(aT[:, par].rearrange("p a b -> p (a b)"), ps[:, par, :], ACT.Copy).then_inc(a_out, 1)
                act.wait_ge(ao_mm, j + 1)
                st.do(act.activation(rope_tmp[:, par * P:(par + 1) * P], ps[:, 2 + par, 0:P], ACT.Square,
                                     accum_out=a_small[:, par, 4:5]))
                st.settle()
                act.activation(a_small[:, par, 4:5], a_small[:, par, 4:5], ACT.Sqrt, scale=1.0 / P,
                               bias=eps[:, 0:1]).then_inc(ao_sq, 1)

            def mlp(i):
                turn_norm(f"n_m{i}")
                L = L_up[i]
                for c in range(8):
                    h = hidT[:, 4 * c:4 * c + 4, :]
                    copy_features(L, c, h, ACT.Relu)
                    act.wait_ge(bank_free, L.e0 + c + 3)
                    act.activation(h, h, ACT.Square).then_inc(hid, 1)
                L = L_down[i]
                for c in range(2):
                    act.wait_ge(ring_done, L.g0 + 4 * c + 3 + 3)
                    e = L.e0 + c
                    act.activation(yM[:, :, c * CW:(c + 1) * CW], ps[:, 2 * (e % 2):2 * (e % 2) + 2, :],
                                   ACT.Copy).then_inc(bank_free, 1)
                root(2)

            act.wait_ge(lam_sums, 1)
            act.activation(lb[:, :, :, :], lb[:, :, :, :], ACT.Exp).then_inc(lam_exps, 1)
            wall_at(act, 0)
            for m, name in ((0, "n_c0"), (1, "n_x0")):
                turn_norm(name)
                mixer(m)
                wall_at(act, 1 + m)
            for p, name in ((0, "p_c0"), (1, "p_x0")):
                turn_norm(name)
                peer(p)
                wall_at(act, 3 + 2 * p)
                peer_gelu(p)
                wall_at(act, 4 + 2 * p)
            turn_norm("n_c1")
            mixer(2)
            wall_at(act, 7)
            turn_norm("n_x1")
            mixer(3)
            wall_at(act, 8)
            turn_norm("p_x1")
            peer(2)
            wall_at(act, 9)
            peer_gelu(2)
            root(0)
            wall_at(act, 10)
            turn_norm("n_kv")
            for c, dst in enumerate((kcN[:, :, 0:CW], kcN[:, :, CW:D], vN[:, 0:NT, 0:CW], vN[:, 0:NT, CW:D])):
                copy_tokens(L_kv, c, dst)
            turn_norm("n_q")
            for c, dst in enumerate((qN[:, :, 0:CW], qN[:, :, CW:D], kxN[:, :, 0:CW], kxN[:, :, CW:D],
                                     vN[:, NT:, 0:CW], vN[:, NT:, CW:D])):
                copy_tokens(L_qkv, c, dst)
            act.wait_ge(lam_sums, 2)
            act.activation(stat[:, 8:10], stat[:, 8:10], ACT.Exp).then_inc(lam_exps, 1)
            turn("q", qT)
            turn("kc", kT[:, :, 0:T])
            turn("kx", kT[:, :, T:2 * T])
            attention()
            turn("ao", hT)
            for c in range(2):
                copy_tokens(L_ao, c, yA[:, :, c * CW:(c + 1) * CW])
            root(2)
            wall_at(act, 11)
            mlp(0)
            wall_at(act, 12)
            act.wait_ge(tab_in, 16 * (N_ATT_TABS + N_HY_TABS))
            act.wait_ge(f_arg, 1)
            for j in range(3):
                act.wait_ge(f_mm, j + 1)
                act.activation(f_x[0:ORDER, :], ps[0:ORDER, 4, 0:T], ACT.Identity, scale=f_b[0:ORDER, 3:4],
                               bias=f_b[0:ORDER, 4 + j:5 + j]).then_inc(f_lin, 1)
                act.wait_ge(f_red, j + 1)
                act.activation(f_hid[0:ORDER, :], f_x[0:ORDER, :], ACT.Sin).then_inc(f_sin, 1)

            def spectrum(dst, n):
                for part in range(2):
                    act.wait_ge(k_mm, 2 * n + part + 1)
                    act.activation(dst[:, part].rearrange("p t (c d) -> p (t c) d", c=2), ps[:, 4:8, :],
                                   ACT.Copy).then_inc(k_out, 1)

            spectrum(Kf, 0)
            wall_at(act, 13)
            turn_norm("n_h")
            for c in range(6):
                chunk_there(L_hin, c)
                e = L_hin.e0 + c
                for b in range(4):
                    j = 4 * c + b
                    ins = act.activation(zT[:, j, :], ps[:, 2 * (e % 2) + b // 2, (b % 2) * T:(b % 2 + 1) * T],
                                         ACT.Identity, bias=hyb[:, j:j + 1])
                ins.then_inc(bank_free, 1)
            r = turn_no["vv"]
            for q in range(4):
                act.wait_ge(tr_done, 4 * r + q + 1)
                act.activation(vNat[:, q // 2, (q % 2) * 512:(q % 2 + 1) * 512], ps[:, 4 + q, :], ACT.Copy).then_inc(tr_out, 1)
            spectrum(Vf, 1)
            root(2)
            wall_at(act, 14)
            mlp(1)
            wall_at(act, 15)

        @block.vector
        def _(dve):
            st = Steps(dve, dve_step)
            roots = [0]
            dve.sem_inc(axpy_done, SLOTS)
            dve.wait_ge(consts_in, 16 * N_CONSTS)
            st.do(dve.tensor_tensor(oml[:, 0], lb[:, 0], lb[:, 1], ALU.max))
            st.settle()
            st.do(dve.tensor_tensor(lb[:, 0], lb[:, 0], oml[:, 0], ALU.subtract))
            dve.tensor_tensor(lb[:, 1], lb[:, 1], oml[:, 0], ALU.subtract).then_inc(lam_sums, 1)
            dve.wait_ge(lam_exps, 1)
            st.do(dve.tensor_tensor(oml[:, 0], lb[:, 0], lb[:, 1], ALU.add))
            st.settle()
            st.do(dve.reciprocal(oml[:, 1], oml[:, 0]))
            st.settle()
            st.do(dve.tensor_tensor(lb[:, 0], lb[:, 0], oml[:, 1], ALU.mult))
            st.do(dve.tensor_tensor(lb[:, 1], lb[:, 1], oml[:, 1], ALU.mult))
            st.settle()
            st.do(dve.tensor_tensor(lb[:, 1], lb[:, 0], lb[:, 1], ALU.add))
            st.settle()
            st.do(dve.tensor_tensor(lb[:, 1], lb[:, 1], lb[:, 0], ALU.subtract))
            st.settle()
            st.do(dve.tensor_tensor(lb[:, 0], lb[:, 0], lb[:, 0], ALU.subtract))
            st.settle()
            st.do(dve.tensor_scalar(oml[:, :], lb[:, :], -1.0, 1.0, ALU.mult, ALU.add))
            for l in range(4):
                L = L_mod[l]
                with dve.Fori(0, L.n // 2) as i:
                    for u in range(2):
                        dve.wait_ge(ring_done, i * 2 + (L.g0 + u + 3))
                        o = mod_row[0:2, l, bass.ds(i * (2 * CW) + u * CW, CW)]
                        dve.tensor_tensor(o, ps[0:2, 2 * ((L.e0 + u) % 2), :], o, ALU.add).then_inc(bank_free, 1)
            wall_at(dve, 0)

            def rms(src, col):
                for t in range(NT):
                    ins = dve.tensor_tensor_reduce(hN[:, t, :], src[:, t, :], src[:, t, :], 1.0 / D, 0.0, ALU.mult,
                                                   ALU.add, stat[:, col + t:col + t + 1])
                ins.then_inc(ms_ready, 1)
                roots[0] += 1
                dve.wait_ge(root_ready, roots[0])
                st.do(dve.reciprocal(stat[:, col:col + NT], stat[:, col:col + NT]))
                st.settle()

            def norm(name, src):
                rms(src, 0)
                dve.wait_ge(vec_full, rows_in[name])
                st.do(dve.scalar_tensor_tensor(vec[:, SCALE, :], vec[:, SCALE, :], 1.0, vec[:, GAIN, :], ALU.add, ALU.mult))
                st.settle()
                for t in range(NT):
                    st.do(dve.scalar_tensor_tensor(hN[:, t, :], src[:, t, :], stat[:, t:t + 1], vec[:, SCALE, :],
                                                   ALU.mult, ALU.mult))
                st.settle()
                for t in range(NT):
                    dve.tensor_tensor(hN[:, t, :], hN[:, t, :], vec[:, SHIFT, :], ALU.add).then_inc(normed, 1)
                dve.wait_ge(normed, NT * (norm_no[name] + 1))
                dve.sem_inc(vec_used, 1)

            def gated(name, L, dst):
                dve.wait_ge(vec_full, rows_in[name])
                for c in range(2):
                    cols = slice(c * CW, (c + 1) * CW)
                    e = L.e0 + c
                    dve.wait_ge(ring_done, L.g0 + c + 3)
                    st.do(dve.tensor_tensor(hN[:, 0, cols], ps[:, 2 * (e % 2), :], vec[:, GATE, cols], ALU.mult))
                    dve.tensor_tensor(hN[:, 1, cols], ps[:, 2 * (e % 2) + 1, :], vec[:, GATE, cols],
                                      ALU.mult).then_inc(bank_free, 1)
                dve.wait_ge(bank_free, L.e0 + 2 + 2)
                for t in range(NT):
                    ins = dve.tensor_tensor(dst[:, t, :], dst[:, t, :], hN[:, t, :], ALU.add)
                    if t < NT - 1:
                        st.do(ins)
                ins.then_inc(resid, 1)
                dve.wait_ge(resid, resid_no[name] + 1)
                dve.sem_inc(vec_used, 1)

            def post(name, y, bias=False):
                dve.wait_ge(vec_full, rows_in[name])
                rms(y, 2)
                st.do(dve.tensor_tensor(vec[:, GAIN, :], vec[:, GAIN, :], vec[:, GATE, :], ALU.mult))
                st.settle()
                for t in range(NT):
                    st.do(dve.scalar_tensor_tensor(hN[:, t, :], y[:, t, :], stat[:, 2 + t:3 + t], vec[:, GAIN, :],
                                                   ALU.mult, ALU.mult))
                st.settle()
                for t in range(NT):
                    ins = dve.tensor_tensor(xs[:, t, :], xs[:, t, :], hN[:, t, :], ALU.add)
                    if t < NT - 1:
                        st.do(ins)
                ins.then_inc(resid, 1)
                dve.wait_ge(resid, resid_no[name] + 1)
                dve.sem_inc(vec_used, 1)

            def flat(b):
                return b.rearrange("p h t -> p (h t)")

            def scan_update(l, queries, last):
                B = 1 << l

                def halves(b):
                    v = flat(b).rearrange("p (n two b) -> p n two b", two=2, b=B)
                    return v[:, :, 0, :], v[:, :, 1, :]

                n = HEADS * T // (2 * B)
                now = [flat(SF), flat(SB)] if l == 0 else [tots[0][l - 1], tots[1][l - 1]]
                pairs = [v.rearrange("p (n two) -> p n two", two=2) for v in now]

                def spread(d, side):
                    return pairs[d][:, :, side:side + 1].to_broadcast([P, n, B])

                todo = []
                if queries:
                    todo += [(halves(QF)[1], spread(0, 0)), (halves(QB)[0], spread(1, 1))]
                todo += [(halves(KF)[0], spread(0, 1)), (halves(KB)[1], spread(1, 0))]
                for d in range(2):
                    st.do(dve.tensor_tensor(tots[d][l], pairs[d][:, :, 0], pairs[d][:, :, 1], ALU.mult))
                for j, (b, f) in enumerate(todo):
                    ins = dve.tensor_tensor(b, b, f, ALU.mult)
                    if j < len(todo) - 1:
                        st.do(ins)
                last(ins)

            def mixer(m):
                L = L_in[m]
                l = 0 if m < 2 else 1
                for d, (s, k) in enumerate(((SF, KF), (SB, KB))):
                    dve.wait_ge(bank_free, L.e0 + 1 + d + 3)
                    for h in range(HEADS):
                        o1, l1 = oml[:, l, d, h:h + 1], lb[:, l, d, h:h + 1]
                        st.do(dve.tensor_scalar(s[:, h, :], s[:, h, :], o1, l1, ALU.mult, ALU.add))
                        st.do(dve.tensor_scalar(k[:, h, :], k[:, h, :], o1, None, ALU.mult))
                st.settle()
                st.do(dve.tensor_scalar(flat(SF), flat(SF), FLOOR, None, ALU.max))
                st.do(dve.tensor_scalar(flat(SB), flat(SB), FLOOR, None, ALU.max))
                st.settle()
                if m == 2:
                    for lev in range(LEVELS):
                        if lev < LEVELS - 1:
                            scan_update(lev, False, st.do)
                            st.settle()
                        else:
                            scan_update(lev, False, lambda ins: ins.then_inc(scan_ready, 1))
                    return
                n = {0: 0, 1: 1, 3: 2}[m]
                dve.wait_ge(bank_free, L.e0 + 3 + 3)
                dve.tensor_tensor(flat(KS), flat(KF), flat(KB), ALU.add).then_inc(lev_ready, 1)
                st.do(dve.tensor_tensor(flat(QF), flat(Q), flat(SF), ALU.mult))
                st.do(dve.tensor_tensor(flat(QB), flat(Q), flat(SB), ALU.mult))
                dve.wait_ge(lev_mm, 9 * n + 1)
                for t in range(NT):
                    ins = dve.tensor_tensor(att[:, t, :, t * P:(t + 1) * P],
                                            ps[:, 4 + t, :].rearrange("p (h t) -> p h t", h=HEADS),
                                            ident[:, :].unsqueeze(1).to_broadcast([P, HEADS, P]), ALU.mult)
                    if t < NT - 1:
                        st.do(ins)
                ins.then_inc(lev_ready, 1)
                for j in range(1, 8):
                    lev = j - 1
                    dve.wait_ge(lev_mm, 9 * n + j + 1)
                    for d in range(2):
                        for t in range(NT):
                            st.do(dve.copy_predicated(
                                att[:, t, :, t * P:(t + 1) * P],
                                masks[:, 7 * d + lev, :].bitcast(U32).unsqueeze(1).to_broadcast([P, HEADS, P]),
                                ps[:, 4 + 2 * d + t, :].rearrange("p (h t) -> p h t", h=HEADS)))
                        st.settle()
                    scan_update(lev, True, lambda ins: ins.then_inc(lev_ready, 1))
                    dve.wait_ge(lev_ready, 9 * n + j + 2)
                dve.wait_ge(lev_mm, 9 * n + 9)
                for st_, b in ((0, 4), (1, 5)):
                    o = slice((1 - st_) * P, (2 - st_) * P)
                    st.do(dve.tensor_copy(att[:, st_, :, o], ps[:, b, :].rearrange("p (h t) -> p h t", h=HEADS)))
                scan_update(LEVELS - 1, True, lambda ins: ins.then_inc(scan_ready, 1))

                dve.wait_ge(bank_free, L.e0 + 7 + 3)
                st.do(dve.tensor_tensor(flat(CU), flat(CG), flat(HV), ALU.mult))
                st.settle()
                for b in range(HEADS):
                    st.do(dve.tensor_scalar(mixT[:, 4 + b, :], CU[:, b, :], convc[:, l, b, 1:2], None, ALU.mult))
                st.settle()
                for tap, sign in ((0, -1), (2, 1)):
                    for b in range(HEADS):
                        w = convc[:, l, b, tap:tap + 1]
                        y, u = mixT[:, 4 + b, :], CU[:, b, :]
                        if m == 0:
                            y, u, hop, size = y.unsqueeze(1), u.unsqueeze(1), 1, T
                        elif b < 2:
                            y, u = [v.rearrange("p (r c) -> p r c", c=GRID_W) for v in (y, u)]
                            hop, size = 1, GRID_W
                        else:
                            y, u, hop, size = y.unsqueeze(1), u.unsqueeze(1), GRID_W, T
                        to = slice(hop, size) if sign < 0 else slice(0, size - hop)
                        fr = slice(0, size - hop) if sign < 0 else slice(hop, size)
                        st.do(dve.scalar_tensor_tensor(y[:, :, to], u[:, :, fr], w, y[:, :, to], ALU.mult, ALU.add))
                    st.settle()
                st.do(dve.tensor_tensor(mixT[:, 4:8, :], mixT[:, 4:8, :], BG, ALU.mult))

                dve.wait_ge(o_root, n + 1)
                st.do(dve.reciprocal(flat(ORS), flat(ORS)))
                st.settle()
                st.do(dve.tensor_tensor(flat(ORS), flat(ORS), flat(G), ALU.mult))
                st.settle()
                dve.tensor_tensor(mixT[:, 0:4, :].rearrange("p h t -> p (h t)"),
                                  ps[:, 4:6, :].rearrange("p a b -> p (a b)"), flat(ORS), ALU.mult).then_inc(mix_ready, 1)

            def top16(values, index, work, source, n):
                for j in range(n):
                    st.do(dve.max(values(j)[:, 0:8], source(j)))
                st.settle()
                for j in range(n):
                    st.do(dve.max_index(index(j)[:, 0:8], values(j)[:, 0:8], source(j)))
                    st.do(dve.match_replace(work(j), values(j)[:, 0:8], source(j), NEG))
                st.settle()
                for j in range(n):
                    st.do(dve.max(values(j)[:, 8:16], work(j)))
                st.settle()
                for j in range(n):
                    st.do(dve.max_index(index(j)[:, 8:16], values(j)[:, 8:16], work(j)))
                st.settle()

            def peer(p):
                l = p // 2
                for t in range(NT):
                    dve.wait_ge(score_out, NT * p + t + 1)
                    top16(lambda j: vals[:, j // 2, j % 2, :], lambda j: vidx[:, j // 2, j % 2, :],
                          lambda j: wk[:, j, :], lambda j: sc[:, t, j, :], 2 * PH)
                    st.do(dve.tensor_copy(vidx_f, vidx))
                    st.do(dve.tensor_tensor(cand, vals[:, :, 0, :].unsqueeze(3).to_broadcast([P, PH, TOPK, TOPK]),
                                            vals[:, :, 1, :].unsqueeze(2).to_broadcast([P, PH, TOPK, TOPK]), ALU.add))
                    st.settle()
                    candr = cand.rearrange("p h a b -> p h (a b)")
                    top16(lambda j: top[:, t, j, :], lambda j: pos[:, j, :], lambda j: cwk[:, j, :],
                          lambda j: candr[:, j, :], PH)
                    posr = pos.rearrange("p h k -> p (h k)")
                    st.do(dve.tensor_scalar(pos2[:, 0, :], posr, 4, None, ALU.logical_shift_right))
                    st.do(dve.tensor_scalar(pos2[:, 1, :], posr, TOPK - 1, None, ALU.bitwise_and))
                    st.settle()
                    st.do(dve.tensor_copy(pos_f, pos2))
                    st.settle()
                    for half in range(2):
                        st.do(dve.tensor_tensor(eqs, pos_f[:, half, :].unsqueeze(2).to_broadcast([P, NSEL, TOPK]),
                                                iota16[:, :].unsqueeze(1).to_broadcast([P, NSEL, TOPK]), ALU.is_equal))
                        st.settle()
                        eq4 = eqs.rearrange("p (h k) a -> p h k a", h=PH)
                        st.do(dve.tensor_tensor(eq4, eq4, vidx_f[:, :, half, :].unsqueeze(2).to_broadcast([P, PH, TOPK, TOPK]),
                                                ALU.mult))
                        st.settle()
                        st.do(dve.reduce_sum(sel[:, half, :], eqs, AX))
                        st.settle()
                    st.do(dve.tensor_scalar(eidx_f[:, t, :], sel[:, 0, :], float(PK), float(l * NEXP), ALU.mult, ALU.add))
                    st.settle()
                    st.do(dve.tensor_tensor(eidx_f[:, t, :], eidx_f[:, t, :], sel[:, 1, :], ALU.add))
                    st.settle()
                    st.do(dve.tensor_copy(eidx[:, t, :], eidx_f[:, t, :]))
                topr = top.rearrange("p t h k -> p (t h) k")
                gr = gates.rearrange("p t (h k) -> p (t h) k", h=PH)
                st.do(dve.tensor_copy(zsum.rearrange("p t h -> p (t h)"), topr[:, :, 0]))
                st.settle()
                zs = zsum.rearrange("p t h -> p (t h)").unsqueeze(2).to_broadcast([P, NT * PH, TOPK])
                dve.tensor_tensor(topr, topr, zs, ALU.subtract).then_inc(gate_sub, 1)
                dve.wait_ge(gate_exp, p + 1)
                st.do(dve.reduce_sum(zsum.rearrange("p t h -> p (t h)"), topr, AX))
                st.settle()
                st.do(dve.reciprocal(zsum, zsum))
                st.settle()
                st.do(dve.tensor_tensor(gr, topr, zs, ALU.mult))
                st.settle()

            def peer_sum(p, name, dst):
                for t in range(NT):
                    K = NT * p + t
                    base = SLOTS + K * (NSEL + 2) + 2
                    for j in range(2):
                        dve.memset(acc[:, j, :], 0.0).then_inc(axpy_done, 1)
                    with dve.Fori(0, NSEL // SLOTS) as i:
                        for half in range(SLOTS // GROUP):
                            grp = slice(half * GROUP, (half + 1) * GROUP)
                            for s in range(half * GROUP, (half + 1) * GROUP):
                                dve.wait_ge(u_full[s], i * 16 + 16 * (K * (NSEL // SLOTS) + 1))
                                ins = dve.tensor_tensor_reduce(ubuf[:, s, :], ubuf[:, s, :], hN[:, t, :], 1.0, 0.0, ALU.mult,
                                                               ALU.add, dots[:, s:s + 1])
                            ins.then_inc(dots_ready, 1)
                            n = 2 * K * (NSEL // SLOTS) + half + 1
                            dve.wait_ge(gelu_done, i * 2 + n)
                            dve.tensor_tensor(coef[:, grp], coef[:, grp], gates[:, t, bass.ds(i * SLOTS + half * GROUP, GROUP)],
                                              ALU.mult).then_inc(coef_ready, 1)
                            dve.wait_ge(coef_ready, i * 2 + n)
                            for s in range(half * GROUP, (half + 1) * GROUP):
                                dve.wait_ge(v_full[s], i * 16 + 16 * (K * (NSEL // SLOTS) + 1))
                                dve.wait_ge(axpy_done, i * SLOTS + (base + s - 1))
                                a_ = acc[:, s % 2, :]
                                dve.scalar_tensor_tensor(a_, vbuf[:, s, :], coef[:, s:s + 1], a_, ALU.mult,
                                                         ALU.add).then_inc(axpy_done, 1)
                    dve.wait_ge(axpy_done, base + NSEL)
                    if t == 0:
                        dve.wait_ge(vec_full, rows_in[name])
                    st.do(dve.tensor_tensor(acc[:, 0, :], acc[:, 0, :], acc[:, 1, :], ALU.add))
                    st.settle()
                    st.do(dve.tensor_tensor(acc[:, 0, :], acc[:, 0, :], vec[:, GATE, :], ALU.mult))
                    st.settle()
                    ins = dve.tensor_tensor(dst[:, t, :], dst[:, t, :], acc[:, 0, :], ALU.add)
                    if t < NT - 1:
                        st.do(ins)
                        st.settle()
                ins.then_inc(resid, 1)
                dve.wait_ge(resid, resid_no[name] + 1)
                dve.sem_inc(vec_used, 1)

            for m, name, dst in ((0, "c0", cs), (1, "x0", xs)):
                norm("n_" + name, dst)
                mixer(m)
                gated("r_" + name, L_out[m], dst)
                wall_at(dve, 1 + m)
            for p, name, dst in ((0, "c0", cs), (1, "x0", xs)):
                norm("p_" + name, dst)
                peer(p)
                wall_at(dve, 3 + 2 * p)
                peer_sum(p, "q_" + name, dst)
                wall_at(dve, 4 + 2 * p)
            norm("n_c1", cs)
            mixer(2)
            wall_at(dve, 7)
            norm("n_x1", xs)
            mixer(3)
            gated("r_x1", L_out[3], xs)
            wall_at(dve, 8)
            norm("p_x1", xs)
            peer(2)
            wall_at(dve, 9)
            peer_sum(2, "q_x1", xs)
            rms(xs, 0)
            dve.wait_ge(vec_full, rows_in["final"])
            for t in range(NT):
                ins = dve.scalar_tensor_tensor(xs[:, t, :], xs[:, t, :], stat[:, t:t + 1], vec[:, GAIN, :], ALU.mult, ALU.mult)
                if t < NT - 1:
                    st.do(ins)
            ins.then_inc(resid, 1)
            dve.wait_ge(resid, resid_no["final"] + 1)
            dve.sem_inc(vec_used, 1)
            wall_at(dve, 10)

            dve.wait_ge(ctx2_in, 16)
            norm("n_kv", cs)
            dve.wait_ge(bank_free, L_kv.e0 + 4 + 2)
            norm("n_q", xs)
            dve.wait_ge(tab_in, 16 * N_ATT_TABS)
            for j in range(2):
                ins = dve.tensor_tensor_reduce(lam_tmp[:, j, :], lam_in[:, 2 * j, :], lam_in[:, 2 * j + 1, :], 1.0, 0.0,
                                               ALU.mult, ALU.add, stat[:, 8 + j:9 + j])
                if j == 0:
                    st.do(ins)
            ins.then_inc(lam_sums, 1)
            st.do(dve.tensor_scalar(subln, subln, 1.0 - LAM_INIT, None, ALU.mult))
            for src, e in ((qN, L_qkv.e0 + 1), (kxN, L_qkv.e0 + 3)):
                dve.wait_ge(bank_free, e + 3)
                for t in range(NT):
                    v = src[:, t, :]
                    a4 = v.rearrange("p (h c x f) -> p h c x f", h=2 * AH, c=2, x=2)
                    o4 = rope_tmp.rearrange("p (h c x f) -> p h c x f", h=2 * AH, c=2, x=2)
                    for x in range(2):
                        st.do(dve.tensor_tensor(o4[:, :, :, x, :], a4[:, :, :, 1 - x, :],
                                                sinT[:, t, :, x, :].unsqueeze(1).to_broadcast([P, 2 * AH, 2, 16]), ALU.mult))
                    st.settle()
                    vh = v.rearrange("p (h d) -> p h d", d=AD)
                    st.do(dve.tensor_tensor(vh, vh, cosT[:, t, :].unsqueeze(1).to_broadcast([P, 2 * AH, AD]), ALU.mult))
                    st.settle()
                    dve.tensor_tensor(v, v, rope_tmp, ALU.add).then_inc(heads_in, 1)
                    dve.wait_ge(heads_in, (0 if src is qN else NT) + t + 1)
            dve.wait_ge(lam_exps, 2)
            st.do(dve.tensor_tensor(stat[:, 10:11], stat[:, 8:9], stat[:, 9:10], ALU.subtract))
            st.settle()
            st.do(dve.tensor_scalar(stat[:, 10:11], stat[:, 10:11], -1.0, -LAM_INIT, ALU.mult, ALU.add))
            st.settle()

            def attention_out(j):
                h, t, par = j // NT, j % NT, j % 2
                dve.wait_ge(ao_sq, j + 1)
                r = a_small[:, par, 4:5]
                st.do(dve.reciprocal(r, r))
                st.settle()
                dve.scalar_tensor_tensor(oN[:, t, h * P:(h + 1) * P], ps[:, 2 + par, 0:P], r, subln, ALU.mult,
                                         ALU.mult).then_inc(ao_norm, 1)

            for j in range(NT * AH):
                b, par = 4 + 2 * (j % 2), j % 2
                dve.wait_ge(s_mm, j + 1)
                st.do(dve.tensor_reduce(a_small[:, par, 0:2], ps[:, b:b + 2, :], AX, ALU.max))
                st.settle()
                dve.tensor_scalar(a_small[:, par, 0:2], a_small[:, par, 0:2], -AD ** -0.5, None, ALU.mult).then_inc(s_bias, 1)
                if j >= 1:
                    attention_out(j - 1)
                dve.wait_ge(s_exp, 2 * j + 2)
                st.do(dve.reciprocal(a_small[:, par, 2:4], a_small[:, par, 2:4]))
                st.settle()
                st.do(dve.tensor_scalar(a_small[:, par, 3:4], a_small[:, par, 3:4], stat[:, 10:11], None, ALU.mult))
                st.do(dve.tensor_scalar(prob[:, par, 0, :], prob[:, par, 0, :], a_small[:, par, 2:3], None, ALU.mult))
                st.settle()
                dve.scalar_tensor_tensor(prob[:, par, 0, :], prob[:, par, 1, :], a_small[:, par, 3:4], prob[:, par, 0, :],
                                         ALU.mult, ALU.add).then_inc(a_ready, 1)
            attention_out(NT * AH - 1)
            dve.wait_ge(bank_free, L_ao.e0 + 2 + 2)
            post("o_0", yA)
            wall_at(dve, 11)

            def mlp(i):
                norm(f"n_m{i}", xs)
                dve.wait_ge(bank_free, L_down[i].e0 + 2 + 2)
                post(f"m_{i}", yM)

            mlp(0)
            wall_at(dve, 12)

            dve.wait_ge(tab_in, 16 * (N_ATT_TABS + N_HY_TABS))
            dve.tensor_scalar(f_b[0:ORDER, 4:7], f_b[0:ORDER, 0:3], f_b[0:ORDER, 3:4], None, ALU.mult).then_inc(f_arg, 1)
            hi = float(np.float32(TWO_PI))
            lo = float(np.float32(TWO_PI - np.float64(np.float32(TWO_PI))))
            fx, fn = f_x[0:ORDER, :], f_n[0:ORDER, :]
            for j in range(3):
                dve.wait_ge(f_lin, j + 1)
                st.do(dve.tensor_scalar(fn, fx, 1.0 / TWO_PI, ROUND, ALU.mult, ALU.add))
                st.settle()
                st.do(dve.tensor_scalar(fn, fn, ROUND, None, ALU.subtract))
                st.settle()
                st.do(dve.scalar_tensor_tensor(fx, fn, -hi, fx, ALU.mult, ALU.add))
                st.settle()
                st.do(dve.scalar_tensor_tensor(fx, fn, -lo, fx, ALU.mult, ALU.add))
                st.settle()
                dve.tensor_scalar(fx, fx, -float(np.float32(np.pi)), float(np.float32(np.pi)), ALU.max, ALU.min).then_inc(f_red, 1)
            for t in range(NT):
                dve.wait_ge(f_h, t + 1)
                for part in range(2):
                    ins = dve.tensor_tensor(taps[:, t, part * D:(part + 1) * D],
                                            ps[:, 4 + 2 * part:6 + 2 * part, :].rearrange("p a b -> p (a b)"),
                                            decay[:, t, :], ALU.mult)
                    if part == 0:
                        st.do(ins)
                ins.then_inc(f_taps, 1)
            dve.wait_ge(f_taps, NT)
            st.do(dve.memset(taps[0:1, 0, D:2 * D], 0.0))
            st.settle()
            st.do(dve.tensor_tensor(ytmp, taps[:, :, 0:D], taps[:, :, D:2 * D], ALU.add))
            st.settle()
            st.do(dve.tensor_tensor(taps[:, :, D:2 * D], taps[:, :, D:2 * D], taps[:, :, 0:D], ALU.subtract))
            st.settle()
            dve.tensor_copy(taps[:, :, 0:D], ytmp).then_inc(f_pm, 1)
            wall_at(dve, 13)

            norm("n_h", xs)
            for c in range(6):
                dve.wait_ge(bank_free, L_hin.e0 + c + 3)
                for j in range(4 * c, 4 * c + 4):
                    st.do(dve.tensor_scalar(zc[:, j, :], zT[:, j, :], hysw[:, j, 1:2], hysb[:, j:j + 1], ALU.mult, ALU.add))
                st.settle()
                for tap in (0, 2):
                    to = slice(1, T) if tap == 0 else slice(0, T - 1)
                    fr = slice(0, T - 1) if tap == 0 else slice(1, T)
                    for j in range(4 * c, 4 * c + 4):
                        st.do(dve.scalar_tensor_tensor(zc[:, j, to], zT[:, j, fr], hysw[:, j, tap:tap + 1], zc[:, j, to],
                                                       ALU.mult, ALU.add))
                    st.settle()
            x0, x1, vg = zc[:, 0:8, :], zc[:, 8:16, :], zc[:, 16:24, :]
            dve.tensor_tensor(vg, vg, x1, ALU.mult).then_inc(vv_ready, 1)
            dve.wait_ge(k_out, 4)
            kr, ki, vr, vs = Kf[:, 0], Kf[:, 1], Vf[:, 0], Vf[:, 1]
            st.do(dve.tensor_tensor(Yf[:, 0], vr, kr, ALU.mult))
            st.do(dve.tensor_tensor(ytmp, vs, ki, ALU.mult))
            st.settle()
            st.do(dve.tensor_tensor(Yf[:, 0], Yf[:, 0], ytmp, ALU.add))
            st.do(dve.tensor_tensor(Yf[:, 1], vs, kr, ALU.mult))
            st.settle()
            st.do(dve.tensor_tensor(ytmp, vr, ki, ALU.mult))
            st.settle()
            dve.tensor_tensor(Yf[:, 1], Yf[:, 1], ytmp, ALU.subtract).then_inc(y_freq, 1)
            dve.wait_ge(conv_mm, 1)
            for b in range(KT):
                st.do(dve.scalar_tensor_tensor(vg[:, b, :], vg[:, b, :], hyd[:, b:b + 1],
                                               ps[:, 4 + b // 2, (b % 2) * T:(b % 2 + 1) * T], ALU.mult, ALU.add))
            st.settle()
            dve.tensor_tensor(hT[:, :, :], vg, x0, ALU.mult).then_inc(vv_ready, 1)
            dve.wait_ge(vec_full, rows_in["o_1"])
            for c in range(2):
                cols = slice(c * CW, (c + 1) * CW)
                e = L_hout.e0 + c
                dve.wait_ge(ring_done, L_hout.g0 + c + 3)
                for t in range(NT):
                    ins = dve.tensor_tensor(yH[:, t, cols], ps[:, 2 * (e % 2) + t, :], vec[:, SHIFT, cols], ALU.add)
                    if t < NT - 1:
                        st.do(ins)
                ins.then_inc(bank_free, 1)
            dve.wait_ge(bank_free, L_hout.e0 + 2 + 2)
            post("o_1", yH)
            wall_at(dve, 14)
            mlp(1)
            wall_at(dve, 15)

        @block.gpsimd
        def _(pool):
            st = Steps(pool, pool_step)
            for dst, src in consts:
                pool.dma_start(dst, src).then_inc(consts_in, 16)

            def load_rows(name):
                if stage_no[name]:
                    pool.wait_ge(vec_used, stage_no[name])
                for row, src in rows[name]:
                    pool.dma_start(vec[:, row, :], src.partition_broadcast(P)).then_inc(vec_full, 16)

            def gathers(p):
                for t in range(NT):
                    K = NT * p + t
                    base = SLOTS + K * (NSEL + 2) + 2
                    with pool.Fori(0, NSEL // SLOTS) as i:
                        for s in range(SLOTS):
                            pool.wait_ge(axpy_done, i * SLOTS + (base + s - 7))
                            pool.tensor_copy(idx_col[:, s:s + 1], eidx[:, t, bass.ds(i * SLOTS + s, 1)]).then_inc(idx_ready, 1)
                            pool.wait_ge(idx_ready, i * SLOTS + (K * NSEL + s + 1))
                            pool.sem_inc(gathers_sent, 1)
                            at = bass.IndirectOffsetOnAxis(ap=idx_col[:, s:s + 1], axis=0)
                            pool.indirect_dma_start(ubuf[:, s, :], None, A["peer_u"], at).then_inc(u_full[s], 16)
                            pool.indirect_dma_start(vbuf[:, s, :], None, A["peer_v"], at).then_inc(v_full[s], 16)

            pool.wait_ge(bank_free, L_mod[3].e0 + 12 + 2)
            pool.dma_start(mods.rearrange("l w n -> w l n"), mod_row[0:2]).then_inc(mod_stored, 16)
            pool.wait_ge(mod_stored, 16)
            wall_at(pool, 0)
            for m, name in ((0, "c0"), (1, "x0")):
                load_rows("n_" + name)
                load_rows("r_" + name)
                wall_at(pool, 1 + m)
            for p, name in ((0, "c0"), (1, "x0")):
                load_rows("p_" + name)
                pool.dma_start(subk[:, :, :], A["subkT"][p // 2]).then_inc(subk_in, 16)
                wall_at(pool, 3 + 2 * p)
                load_rows("q_" + name)
                gathers(p)
                wall_at(pool, 4 + 2 * p)
            load_rows("n_c1")
            wall_at(pool, 7)
            load_rows("n_x1")
            load_rows("r_x1")
            wall_at(pool, 8)
            load_rows("p_x1")
            pool.dma_start(subk[:, :, :], A["subkT"][1]).then_inc(subk_in, 16)
            wall_at(pool, 9)
            load_rows("q_x1")
            gathers(2)
            load_rows("final")
            wall_at(pool, 10)
            pool.dma_start(cs[:, :, :], A["ctx_2"].rearrange("(t p) d -> p t d", p=P)).then_inc(ctx2_in, 16)
            for dst, src in att_tabs:
                pool.dma_start(dst, src).then_inc(tab_in, 16)
            for name in ("n_kv", "n_q", "o_0"):
                load_rows(name)
            wall_at(pool, 11)
            for name in ("n_m0", "m_0"):
                load_rows(name)
            wall_at(pool, 12)
            for dst, src in hy_tabs:
                pool.dma_start(dst, src).then_inc(tab_in, 16)
            wall_at(pool, 13)
            for name in ("n_h", "o_1"):
                load_rows(name)
            wall_at(pool, 14)
            for name in ("n_m1", "m_1"):
                load_rows(name)
            wall_at(pool, 15)
            pool.dma_start(out.rearrange("b (t p) d -> p (b t) d", p=P), xs[:, :, :]).then_inc(stored, 16)
            pool.wait_ge(stored, 16)


def tables():
    f32 = np.float32
    c = {"ident": np.eye(P, dtype=f32), "mean_mat": np.full((P, P), 1.0 / P, f32)}
    c["eps"] = np.full((P, 1), EPS, f32)
    s, t = np.meshgrid(np.arange(P), np.arange(P), indexing="ij")
    m = np.zeros((P, 14, P), f32)
    for lev in range(7):
        same = (s >> (lev + 1)) == (t >> (lev + 1))
        m[:, lev] = same & ((s >> lev) % 2 == 0) & ((t >> lev) % 2 == 1)
        m[:, 7 + lev] = same & ((s >> lev) % 2 == 1) & ((t >> lev) % 2 == 0)
    c["masks"] = m
    c["iota16"] = np.tile(np.arange(TOPK, dtype=f32), (P, 1))
    inv = f32(10000.0) ** (-np.arange(16, dtype=f32) / f32(16))
    pos = np.stack([np.arange(T) // GRID_W, np.arange(T) % GRID_W], 1).astype(f32)
    ang = pos[:, :, None] * inv[None, None, :].astype(f32)
    co, si = np.cos(ang).astype(f32), np.sin(ang).astype(f32)
    c["rope_cos"] = np.stack([co, co], 2).reshape(T, AD)
    c["rope_sin"] = np.stack([-si, si], 2).reshape(T, AD)
    n, f = np.meshgrid(np.arange(T), np.arange(T), indexing="ij")
    th = 2.0 * np.pi * ((n * (2 * f + 1)) % (4 * T)) / (4.0 * T)
    c["dft"] = np.stack([np.cos(th), np.sin(th)]).astype(f32)
    c["idft"] = (np.stack([np.cos(th).T, np.sin(th).T]) / T).astype(f32)
    bands = (EMB - 1) // 2
    tt = np.linspace(0.0, 1.0, T, dtype=f32)[:, None]
    w = (f32(2.0 * np.pi) * np.arange(T, dtype=f32)[:, None] / f32(T)).astype(f32)
    fr = np.linspace(1e-4, bands - 1, bands, dtype=f32)[None, :]
    arg = (fr * w).astype(f32)
    c["filt_emb"] = np.ascontiguousarray(np.concatenate([tt, np.cos(arg), -np.sin(arg)], 1).astype(f32).T)
    deltas = np.abs(np.linspace(np.log(1e-2) / 1.5, np.log(1e-2) / 0.3, D, dtype=f32))
    c["decay"] = np.exp(-tt * deltas[None, :]).astype(f32)
    return c


def lay_out(i):
    r = {}

    def blocks(v):
        return np.moveaxis(v.reshape((-1, P) + v.shape[1:]), 0, 1)

    r["x"], r["ctx"], r["ctx_2"] = i["x"][0], i["ctx"][0], i["ctx_2"][0]
    conds = np.stack([i["c"][0], i["c_ctx"], i["c_2"][0], i["c_ctx_2"]], 1)
    r["condT"] = blocks(conds)
    r["w_mod4"] = np.concatenate([i["w_mod"], i["w_mod_2"]])
    r["b_mod4"] = np.concatenate([i["b_mod"], i["b_mod_2"]])
    for k in ("norm1_g", "norm2_g", "final_g", "w_in", "w_out", "peer_wq"):
        r[k] = i[k]
    r["convT"] = np.stack([blocks(w.T) for w in i["conv_w"]], 1)
    lbl = i["lb_logits"]
    r["lbT"] = lbl.reshape(lbl.shape[0], 2, HEADS, P).transpose(3, 0, 1, 2)
    sk = i["peer_subkeys"]
    r["subkT"] = sk.transpose(0, 4, 1, 2, 3).reshape(sk.shape[0], P, 2 * PH, PK)
    r["peer_u"] = i["peer_u"].reshape(-1, D)
    r["peer_v"] = i["peer_v"].reshape(-1, D)
    for k in ("norm_mix_pre", "norm_mix_post", "norm_mlp_pre", "norm_mlp_post", "w_mlp_in", "w_mlp_out"):
        r[k] = i[k + "_2"]
    for k in ("attn_w_qkv", "attn_w_out", "attn_subln", "hy_w_in", "hy_w_out", "hy_b_out",
              "hy_filt_w1", "hy_filt_w2", "hy_filt_w_out"):
        r[k] = i[k + "_2"][0]
    r["attn_lambda"] = i["attn_lambda_2"][0].reshape(-1)
    r["filt_b"] = np.stack([i["hy_filt_b1_2"][0], *i["hy_filt_b2_2"][0], i["hy_filt_freq_2"][0]], 1)
    r["hy_bT"] = blocks(i["hy_b_in_2"][0])
    r["hy_swT"] = blocks(i["hy_w_short_2"][0].T)
    r["hy_sbT"] = blocks(i["hy_b_short_2"][0])
    r["hy_dT"] = blocks(i["hy_bias_2"][0])
    return r


def kernel(**inputs):
    import concourse.bacc as bacc
    from concourse.bass_utils import run_bass_kernel_spmd

    nc = bacc.Bacc("TRN2", target_bir_lowering=False, num_devices=1)
    given = {k: np.asarray(v) for k, v in inputs.items()}
    arrays, A = {}, {}
    for name, v in {**lay_out(given), **tables()}.items():
        v = np.ascontiguousarray(v)
        arrays["in_" + name] = v
        A[name] = nc.dram_tensor("in_" + name, v.shape, mybir.dt.from_np(v.dtype), kind="ExternalInput").ap()
    out = nc.dram_tensor("out", (1, T, D), F32, kind="ExternalOutput").ap()
    program(nc, A, out)
    got = run_bass_kernel_spmd(nc, [arrays], core_ids=[0])
    return got.results[0]["out"]
```

```python
from contextlib import ExitStack

import numpy as np

import concourse.bass as bass
from concourse import mybir
from concourse.alu_op_type import AluOpType as ALU

ACT = mybir.ActivationFunctionType
AX = mybir.AxisListType.X
F32 = mybir.dt.float32
U32 = mybir.dt.uint32
U8 = mybir.dt.uint8

P = 128
T = 256
NT = T // P
D = 1024
KT = D // P
CW = 512
GRID_W = 64
HEADS = 4
HW = 512
LEVELS = 8
PH, PK, TOPK = 8, 128, 16
NSEL = PH * TOPK
NEXP = PK * PK
EPS = 1e-6
FLOOR = 1e-20
NEG = -3.0e38
AH, AD = 8, 64
LAM_INIT = 0.8 - 0.6
FF = 4096
EMB, ORDER = 33, 64
GROUP = 4
NGRP = NSEL // GROUP
ALLGRP = NT * NGRP
TWO_PI = 2.0 * np.pi
ROUND = 1.5 * 2.0 ** 23


class Steps:

    def __init__(self, eng, sem):
        self.eng, self.sem, self.n = eng, sem, 0

    def do(self, ins):
        self.n += 1
        ins.then_inc(self.sem, 1)

    def settle(self):
        self.eng.wait_ge(self.sem, self.n)


class Linear:

    def __init__(self, src, n, g0, e0, gens):
        self.src, self.n, self.g0, self.e0, self.gens = src, n, g0, e0, gens


def program(nc, A, out):
    ctx = ExitStack()

    def sb(name, shape, dt=F32):
        return ctx.enter_context(nc.sbuf_tensor(name, shape, dt))

    def sem(name):
        return ctx.enter_context(nc.semaphore(name))

    with ctx:
        ring = sb("ring", [P, 2, KT, CW])
        xs = sb("xs", [P, NT, D])
        cs = sb("cs", [P, NT, D])
        hA, hB = sb("hA", [P, NT, D]), sb("hB", [P, NT, D])
        hT = sb("hT", [P, KT, T])
        vec = sb("vec", [P, 3, D])
        GAIN, SCALE, SHIFT = range(3)
        GATE = SCALE
        pgate = sb("pgate", [P, D])
        mod_io = sb("mod_io", [P, 2, CW])
        ident = sb("ident", [P, P])
        mean_mat = sb("mean_mat", [P, P])
        masks = sb("masks", [P, 14, P], U8)
        iota16 = sb("iota16", [P, TOPK])
        states = sb("states", [P, 2, HEADS, P])
        lb = sb("lb", [P, 2, 2, HEADS])
        oml = sb("oml", [P, 2, 2, HEADS])
        convc = sb("convc", [P, 2, HEADS, 3])
        condS = sb("condS", [P, KT, 4])
        stat = sb("stat", [P, 16])
        eps = sb("eps", [P, 1])
        ARENA = 27776
        arena = sb("arena", [P, ARENA])
        ps = ctx.enter_context(nc.psum_tensor("ps", [P, 8, 512], F32))
        mods = nc.dram_tensor("mods", [4, 2, 6 * D], F32, kind="Internal").ap()

        class Area:

            def __init__(self):
                self.at = 0

            def take(self, *dims):
                n = int(np.prod(dims))
                flat = arena[:, self.at:self.at + n]
                self.at += n
                assert self.at <= ARENA, self.at
                if len(dims) == 1:
                    return flat
                names = "abcd"[:len(dims)]
                return flat.rearrange(f"p ({' '.join(names)}) -> p {' '.join(names)}",
                                      **{k: v for k, v in zip(names, dims)})

        ring_full = [sem(f"ring_full{s}") for s in range(2)]
        ring_done = sem("ring_done")
        bank_free = sem("bank_free")
        consts_in = sem("consts_in")
        cond_ready = sem("cond_ready")
        bias_in = [sem(f"bias_in{s}") for s in range(2)]
        mod_stored = [sem(f"mod_stored{s}") for s in range(2)]
        masks_in = sem("masks_in")
        vec_full = sem("vec_full")
        vec_used = sem("vec_used")
        normed = sem("normed")
        tr_done = sem("tr_done")
        tr_out = sem("tr_out")
        lev_ready = sem("lev_ready")
        lev_mm = sem("lev_mm")
        scan_ready = sem("scan_ready")
        o_done = sem("o_done")
        o_sq = sem("o_sq")
        o_ms = sem("o_ms")
        o_root = sem("o_root")
        kr_turned = sem("kr_turned")
        kr_out = sem("kr_out")
        st_done = sem("st_done")
        st_out = sem("st_out")
        mix_ready = sem("mix_ready")
        resid = sem("resid")
        subk_in = sem("subk_in")
        score_mm = sem("score_mm")
        score_out = sem("score_out")
        gate_sub = sem("gate_sub")
        gate_exp = sem("gate_exp")
        picks = sem("picks")
        pgate_in = sem("pgate_in")
        peer_out = sem("peer_out")
        idx_ready = sem("idx_ready")
        gathers_sent = sem("gathers_sent")
        u_full = [sem(f"u_full{s}") for s in range(GROUP)]
        v_full = [sem(f"v_full{s}") for s in range(2 * GROUP)]
        dot_done = sem("dot_done")
        gelu_done = sem("gelu_done")
        coef_ready = sem("coef_ready")
        axpy_done = sem("axpy_done")
        ctx2_in = sem("ctx2_in")
        tab_in = sem("tab_in")
        lam_sums = sem("lam_sums")
        lam_exps = sem("lam_exps")
        heads_in = sem("heads_in")
        s_mm = sem("s_mm")
        s_bias = sem("s_bias")
        s_exp = sem("s_exp")
        a_ready = sem("a_ready")
        a_turned = sem("a_turned")
        a_out = sem("a_out")
        ao_mm = sem("ao_mm")
        ao_sq = sem("ao_sq")
        ao_root = sem("ao_root")
        ao_norm = sem("ao_norm")
        y_out = sem("y_out")
        hid = sem("hid")
        f_mm = sem("f_mm")
        f_arg = sem("f_arg")
        f_lin = sem("f_lin")
        f_red = sem("f_red")
        f_sin = sem("f_sin")
        f_h = sem("f_h")
        f_taps = sem("f_taps")
        f_pm = sem("f_pm")
        k_mm = sem("k_mm")
        k_out = sem("k_out")
        vv_ready = sem("vv_ready")
        y_freq = sem("y_freq")
        conv_mm = sem("conv_mm")
        stored = sem("stored")
        wall = sem("wall")
        ms_ready = sem("ms_ready")
        root_ready = sem("root_ready")
        dve_step, act_step, pool_step = sem("dve_step"), sem("act_step"), sem("pool_step")

        plan = []
        place = [0, 0]

        def linear(src, n, gens=None):
            L = Linear(src, n, place[0], place[1], gens or n)
            place[0] += n
            place[1] += L.gens
            plan.append(L)
            return L

        def chunked(w, c0=0):
            v = w.rearrange("(k p) n -> p k n", p=P)
            return lambda c: v[:, :, bass.ds(c * CW + c0 * CW, CW)]

        def chunked_deep(w):
            v = w.rearrange("(g k p) n -> g p k n", k=KT, p=P)
            return lambda c: v[c % 4, :, :, (c // 4) * CW:(c // 4 + 1) * CW]

        L_mod, L_in, L_out, L_wq = {}, {}, {}, {}
        IN_ORDER = [1, 2, 3, 0, 5, 7, 6, 4]

        def plan_mod(l):
            L_mod[l] = linear(chunked(A["w_mod4"][l]), 12)

        def plan_in(m, l, order):
            w = chunked(A["w_in"][l])
            L_in[m] = linear(lambda c: w(order[c]), len(order))

        def plan_out(m, l):
            L_out[m] = linear(chunked(A["w_out"][l]), 2)

        def plan_wq(p, l):
            L_wq[p] = linear(chunked(A["peer_wq"][l]), 4)

        plan_mod(0)
        plan_in(0, 0, IN_ORDER), plan_out(0, 0), plan_wq(0, 0)
        plan_mod(1)
        plan_in(1, 0, IN_ORDER), plan_out(1, 0), plan_wq(1, 0)
        plan_mod(2), plan_in(2, 1, [1, 2, 0])
        plan_in(3, 1, IN_ORDER), plan_out(3, 1), plan_wq(2, 1)
        plan_mod(3)
        L_kv = linear(chunked(A["attn_w_qkv"], 2), 4)
        L_qkv = linear(chunked(A["attn_w_qkv"]), 6)
        L_ao = linear(chunked(A["attn_w_out"]), 2)
        L_up, L_down = {}, {}
        L_up[0] = linear(chunked(A["w_mlp_in"][0]), 8)
        L_down[0] = linear(chunked_deep(A["w_mlp_out"][0]), 8, 2)
        L_hin = linear(chunked(A["hy_w_in"]), 6)
        L_hout = linear(chunked(A["hy_w_out"]), 2)
        L_up[1] = linear(chunked(A["w_mlp_in"][1]), 8)
        L_down[1] = linear(chunked_deep(A["w_mlp_out"][1]), 8, 2)

        def mod(l, who, j):
            return mods[l, who, j * D:(j + 1) * D]

        def pre(l, who, g, j):
            return [(GAIN, g), (SHIFT, mod(l, who, j)), (SCALE, mod(l, who, j + 1))]

        X, C = 0, 1
        rows = {}
        rows["n_c0"] = pre(0, C, A["norm1_g"][0], 0)
        rows["r_c0"] = [(GATE, mod(0, C, 2))]
        rows["p_c0"] = pre(0, C, A["norm2_g"][0], 3)
        rows["n_x0"] = pre(0, X, A["norm1_g"][0], 0)
        rows["r_x0"] = [(GATE, mod(0, X, 2))]
        rows["p_x0"] = pre(0, X, A["norm2_g"][0], 3)
        rows["n_c1"] = pre(1, C, A["norm1_g"][1], 0)
        rows["n_x1"] = pre(1, X, A["norm1_g"][1], 0)
        rows["r_x1"] = [(GATE, mod(1, X, 2))]
        rows["p_x1"] = pre(1, X, A["norm2_g"][1], 3)
        rows["n_kv"] = pre(2, C, A["norm_mix_pre"][0], 0)
        rows["final"] = [(GAIN, A["final_g"])]
        rows["n_q"] = pre(2, X, A["norm_mix_pre"][0], 0)
        rows["o_0"] = [(GAIN, A["norm_mix_post"][0]), (GATE, mod(2, X, 2))]
        rows["n_m0"] = pre(2, X, A["norm_mlp_pre"][0], 3)
        rows["m_0"] = [(GAIN, A["norm_mlp_post"][0]), (GATE, mod(2, X, 5))]
        rows["n_h"] = pre(3, X, A["norm_mix_pre"][1], 0)
        rows["o_1"] = [(GAIN, A["norm_mix_post"][1]), (GATE, mod(3, X, 2)), (SHIFT, A["hy_b_out"])]
        rows["n_m1"] = pre(3, X, A["norm_mlp_pre"][1], 3)
        rows["m_1"] = [(GAIN, A["norm_mlp_post"][1]), (GATE, mod(3, X, 5))]
        stage_no, rows_in, total = {}, {}, 0
        for j, (name, rs) in enumerate(rows.items()):
            stage_no[name] = j
            total += 16 * len(rs)
            rows_in[name] = total
        norm_order = [s for s in rows if s[0] in "np" and s != "final"]
        norm_buf = {s: hB if s in ("n_x0", "p_x0", "n_kv") else hA for s in norm_order}
        norm_no = {s: j for j, s in enumerate(norm_order)}

        turn_no = {s: j for j, s in enumerate(
            ["n_c0", "p_c0", "n_x0", "p_x0", "n_c1", "n_x1", "p_x1", "n_kv", "kc", "n_q", "q", "kx", "ao",
             "n_m0", "n_h", "vv", "n_m1"])}

        resid_no = {s: j for j, s in enumerate(
            ["r_c0", "r_x0", "r_x1", "final", "o_0", "m_0", "o_1", "m_1"])}
        PEER_GATE = [mod(0, C, 5), mod(0, X, 5), mod(1, X, 5)]

        PARTS = 4
        HQ, NQ = PH // PARTS, NSEL // PARTS
        SETS = 4

        MAIN = 13 * 1024
        a = Area()
        mask_f = a.take(14, P)

        a = Area()
        SF, KF, SB, KB, Q, QF, QB, G, CG, BG = [a.take(HEADS, T) for _ in range(10)]
        HV = Q
        OSQ, ORS = SF, SB
        att = a.take(NT, HEADS, T)
        ivN = a.take(NT, HW)
        mixT = hT
        KRN = arena[:, 5 * 1024:7 * 1024].rearrange("p (d s h k) -> p d s h k", d=2, s=NT, h=HEADS)
        assert a.at <= MAIN

        a = Area()
        qrT = a.take(2 * PH, T)
        subk = a.take(2 * PH, PK)
        sc = a.take(2 * PH, PK)
        eqs = sc.rearrange("p j k -> p (j k)").rearrange("p (n a) -> p n a", a=TOPK)
        cand = a.take(PH, TOPK, TOPK)
        vals = a.take(PH, 2, TOPK)
        vidx = a.take(PH, 2, TOPK).bitcast(U32)
        vidx_f = a.take(PH, 2, TOPK)
        top = a.take(PH, TOPK)
        pos = a.take(PH, TOPK).bitcast(U32)
        pos2 = a.take(2, NSEL).bitcast(U32)
        pos_f = a.take(2, NSEL)
        sel = a.take(2, NSEL)
        eidx_f = a.take(NSEL)
        zsum = a.take(PH)
        assert a.at <= MAIN

        a = Area()
        a.at = MAIN
        gates = a.take(2, NT, NSEL)
        eidx = a.take(2, NT, NSEL).bitcast(U32)
        ubuf = a.take(GROUP, D)
        vbuf = a.take(2 * GROUP, D)
        acc = a.take(D)
        dots = a.take(2 * GROUP)
        coef = a.take(2 * GROUP)
        row_no = a.take(SETS, GROUP).bitcast(U32)

        a = Area()
        kcN = a.take(NT, D)
        vN = a.take(2 * NT, D)
        kT = a.take(AH, 2 * T)
        assert a.at <= MAIN
        qN, kxN = a.take(NT, D), a.take(NT, D)
        qT = a.take(AH, T)
        prob = a.take(2, 2, 2 * T)
        aT = a.take(2, 4, P)
        oN = a.take(NT, D)
        rope_tmp = a.take(D)
        cosT, sinT = a.take(NT, AD), a.take(NT, 2, 2, 16)
        subln = a.take(P)
        lam_in = a.take(4, AD)
        lam_tmp = a.take(2, AD)
        a_small = a.take(2, 8)
        ao_ms = a.take(NT * AH)
        yA = oN

        a = Area()
        hidT = a.take(FF // P, T)
        yM = a.take(NT, D)

        a = Area()
        zT = a.take(24, T)
        zc = a.take(24, T)
        Kf = a.take(2, NT, D)
        Vf = a.take(2, NT, D)
        vNat = a.take(NT, D)
        dft = a.take(2, NT, T)
        idft = a.take(2, NT, T)
        hyb = a.take(24)
        hysw = a.take(24, 3)
        hysb = a.take(24)
        hyd = a.take(KT)
        taps = zT.rearrange("p a b -> p (a b)")[:, 0:NT * 2 * D].rearrange("p (t d) -> p t d", t=NT)
        decay = zc.rearrange("p a b -> p (a b)")[:, 0:NT * D].rearrange("p (t d) -> p t d", t=NT)
        f_out = zc.rearrange("p a b -> p (a b)")[:, NT * D:2 * NT * D]
        zrest = zc.rearrange("p a b -> p (a b)")[:, 2 * NT * D:3 * NT * D]
        f_emb, f_hid = zrest[:, 0:T], zrest[:, T:2 * T]
        f_x, f_n = zrest[:, 2 * T:3 * T], zrest[:, 3 * T:4 * T]
        f_w = zrest[:, 4 * T:4 * T + 3 * ORDER].rearrange("p (j o) -> p j o", j=3)
        f_b = zrest[:, 5 * T:5 * T + 8]
        Yf = zT.rearrange("p a b -> p (a b)")[:, 0:2 * NT * D].rearrange("p (c t d) -> p c t d", c=2, t=NT)
        ytmp = zT.rearrange("p a b -> p (a b)")[:, 2 * NT * D:3 * NT * D].rearrange("p (t d) -> p t d", t=NT)
        yH = Vf[:, 0]

        consts = [
            (mask_f, A["masks"]), (ident[:, :], A["ident"]), (mean_mat[:, :], A["mean_mat"]), 
            (eps[:, :], A["eps"]), (iota16[:, :], A["iota16"]), (lb[:, :, :, :], A["lbT"]),
            (convc[:, :, :, :], A["convT"]), (condS[:, :, :], A["condT"]),
            (cs[:, :, :], A["ctx"].rearrange("(t p) d -> p t d", p=P)),
            (xs[:, :, :], A["x"].rearrange("(t p) d -> p t d", p=P)),
        ]
        N_CONSTS = len(consts)
        att_tabs = [
            (cosT, A["rope_cos"].rearrange("(t p) d -> p t d", p=P)),
            (sinT.rearrange("p t c x f -> p t (c x f)"), A["rope_sin"].rearrange("(t p) d -> p t d", p=P)),
            (subln, A["attn_subln"].partition_broadcast(P)),
            (lam_in.rearrange("p a d -> p (a d)"), A["attn_lambda"].partition_broadcast(P)),
        ]
        N_ATT_TABS = len(att_tabs)
        hy_tabs = [
            (dft, A["dft"].rearrange("c (t p) f -> p c t f", p=P)),
            (idft, A["idft"].rearrange("c (t p) f -> p c t f", p=P)),
            (decay, A["decay"].rearrange("(t p) d -> p t d", p=P)),
            (f_out[0:ORDER, :], A["hy_filt_w_out"]), (f_emb[0:EMB, :], A["filt_emb"]),
            (f_w[0:EMB, 0, :], A["hy_filt_w1"]), (f_w[0:ORDER, 1:3, :], A["hy_filt_w2"].rearrange("j i o -> i j o")),
            (f_b[0:ORDER, 0:4], A["filt_b"]),
            (hyb, A["hy_bT"]), (hysw, A["hy_swT"]), (hysb, A["hy_sbT"]), (hyd, A["hy_dT"]),
        ]
        N_HY_TABS = len(hy_tabs)

        block = ctx.enter_context(nc.Block())

        def run(*stages):
            for stage in stages:
                for _ in stage:
                    pass

        RATE = (6, 5), (1, 1), (6, 5)

        def blend(parts, others):
            n = 0
            for part in parts:
                for _ in part:
                    yield
                    n += 1
                    if n % 3 == 0 and next(others, others) is not others:
                        yield
            for _ in others:
                yield

        def weave(p, rate, segment, segments, *stages):
            pieces = (x for stage in stages for x in stage)
            more, g, due = True, 0, 0
            while g <= ALLGRP:
                plain = NGRP - g % NGRP if g % NGRP >= 2 else 0
                if more or plain < 2:
                    segment(p, g)
                    g += 1
                    due += rate[0]
                    while more and due >= rate[1]:
                        due -= rate[1]
                        more = next(pieces, pieces) is not pieces
                else:
                    n = plain // 2 * 2
                    segments(p, g, n)
                    g += n
            run(pieces)

        def wall_at(eng, n):
            eng.drain().then_inc(wall, 1)
            eng.wait_ge(wall, 4 * (n + 1))

        @block.sync
        def _(sp):
            def chunk(L, c, i, u):
                g = L.g0 + u
                sp.wait_ge(ring_done, i * 2 + (g + 1))
                sp.dma_start(ring[:, g % 2], L.src(c)).then_inc(ring_full[g % 2], 16)

            def weights(L):
                if L.gens == L.n and L.n % 4 == 0 and L not in L_in.values():
                    with sp.Fori(0, L.n // 2) as i:
                        for u in range(2):
                            chunk(L, i * 2 + u, i, u)
                else:
                    for c in range(L.n):
                        chunk(L, c, 0, c)

            def load_rows(name):
                if stage_no[name]:
                    sp.wait_ge(vec_used, stage_no[name])
                for row, src in rows[name]:
                    sp.dma_start(vec[:, row, :], src.partition_broadcast(P)).then_inc(vec_full, 16)

            def modulation(l):
                L = L_mod[l]
                with sp.Fori(0, L.n // 2) as i:
                    for u in range(2):
                        chunk(L, i * 2 + u, i, u)
                        sp.wait_ge(mod_stored[u], i * 16 + 16 * (6 * l + 1))
                        sp.dma_start(mod_io[0:2, u, :], A["b_mod4"][l, bass.ds(i * (2 * CW) + u * CW, CW)].partition_broadcast(2)
                                     ).then_inc(bias_in[u], 16)

            def modulated(l):
                for s in range(2):
                    sp.wait_ge(mod_stored[s], 16 * (6 * (l + 1) + 1))

            def peer_weights(name, p):
                load_rows(name)
                sp.dma_start(subk, A["subkT"][p // 2]).then_inc(subk_in, 16)
                weights(L_wq[p])

            modulation(0)
            modulated(0)
            for j, name in enumerate(("c0", "x0")):
                load_rows("n_" + name)
                weights(L_in[j])
                load_rows("r_" + name)
                weights(L_out[j])
                peer_weights("p_" + name, j)
                modulation(j + 1)
            modulated(1)
            load_rows("n_c1")
            weights(L_in[2])
            load_rows("n_x1")
            sp.dma_start(cs[:, :, :], A["ctx_2"].rearrange("(t p) d -> p t d", p=P)).then_inc(ctx2_in, 16)
            weights(L_in[3])
            load_rows("r_x1")
            weights(L_out[3])
            peer_weights("p_x1", 2)
            modulation(3)
            modulated(3)
            load_rows("n_kv")
            weights(L_kv)
            load_rows("final")
            load_rows("n_q")
            weights(L_qkv)
            load_rows("o_0")
            weights(L_ao)
            load_rows("n_m0")
            weights(L_up[0])
            load_rows("m_0")
            weights(L_down[0])
            load_rows("n_h")
            weights(L_hin)
            load_rows("o_1")
            weights(L_hout)
            load_rows("n_m1")
            weights(L_up[1])
            load_rows("m_1")
            weights(L_down[1])

        @block.tensor
        def _(pe):
            pe.sem_inc(ring_done, 2)
            pe.wait_ge(consts_in, 16 * N_CONSTS)

            def enter(L, u, i=0, e=None):
                g = L.g0 + u
                pe.wait_ge(ring_full[g % 2], i * 16 + 16 * (g // 2 + 1))
                if e is not None:
                    pe.wait_ge(bank_free, i * 2 + (e + 1))
                return g % 2

            def tokens_chunk(s, e, lhs, k0=0, first=True, last=True):
                for t in range(NT):
                    for k in range(KT):
                        mm = pe.matmul(ps[:, 2 * (e % 2) + t, :], lhs[:, k0 + k, t * P:(t + 1) * P],
                                       ring[:, s, k, :], start=first and k == 0, stop=last and k == KT - 1)
                mm.then_inc(ring_done, 1)

            def features_chunk(s, e, rhs):
                for b in range(4):
                    o = ps[:, 2 * (e % 2) + b // 2, (b % 2) * T:(b % 2 + 1) * T]
                    for k in range(KT):
                        mm = pe.matmul(o, ring[:, s, k, b * P:(b + 1) * P], rhs[:, k, :],
                                       start=k == 0, stop=k == KT - 1)
                mm.then_inc(ring_done, 1)

            def features(L, rhs, c0=0):
                if L.n - c0 >= 4 and (L.n - c0) % 2 == 0:
                    with pe.Fori(0, (L.n - c0) // 2) as i:
                        for u in range(2):
                            features_chunk(enter(L, c0 + u, i, L.e0 + c0 + u), L.e0 + c0 + u, rhs)
                else:
                    for c in range(c0, L.n):
                        features_chunk(enter(L, c, 0, L.e0 + c), L.e0 + c, rhs)

            def tokens(L, lhs):
                if L.n >= 4:
                    with pe.Fori(0, L.n // 2) as i:
                        for u in range(2):
                            tokens_chunk(enter(L, u, i, L.e0 + u), L.e0 + u, lhs)
                else:
                    for c in range(L.n):
                        tokens_chunk(enter(L, c, 0, L.e0 + c), L.e0 + c, lhs)

            def turn(name, src, ready, value):
                r = turn_no[name]
                for t in range(NT):
                    pe.wait_ge(ready, value(t))
                    if r:
                        pe.wait_ge(tr_out, 4 * r)
                    for half in range(2):
                        for j in range(4):
                            k = 4 * half + j
                            mm = pe.transpose(ps[:, 4 + 2 * t + half, j * P:(j + 1) * P],
                                              src[:, t, k * P:(k + 1) * P], ident[:, :])
                        mm.then_inc(tr_done, 1)

            def turn_norm(name):
                turn(name, norm_buf[name], normed, lambda t: NT * norm_no[name] + t + 1)
                pe.wait_ge(tr_out, 4 * (turn_no[name] + 1))

            def modulation(l):
                L = L_mod[l]
                with pe.Fori(0, L.n // 2) as i:
                    for u in range(2):
                        s, e = enter(L, u, i, L.e0 + u), L.e0 + u
                        o = ps[0:2, 2 * (e % 2), :]
                        for k in range(KT):
                            mm = pe.matmul(o, condS[:, k, 2 * (l // 2):2 * (l // 2) + 2], ring[:, s, k, :],
                                           start=k == 0, stop=k == KT - 1)
                        mm.then_inc(ring_done, 1)

            def mixer(m):
                L = L_in[m]
                n = {0: 0, 1: 1, 3: 2}.get(m)

                def part(c, lo, hi):
                    e = L.e0 + c
                    s = enter(L, c, 0, e) if lo == 0 else (L.g0 + c) % 2
                    if c == (2 if m == 2 else 3):
                        for t in range(lo // 2, hi // 2):
                            for k in range(KT):
                                mm = pe.matmul(ps[:, 2 * (e % 2) + t, :], hT[:, k, t * P:(t + 1) * P], ring[:, s, k, :],
                                               start=k == 0, stop=k == KT - 1)
                    else:
                        for b in range(lo, hi):
                            for k in range(KT):
                                mm = pe.matmul(ps[:, 2 * (e % 2) + b // 2, (b % 2) * T:(b % 2 + 1) * T],
                                               ring[:, s, k, b * P:(b + 1) * P], hT[:, k, :], start=k == 0, stop=k == KT - 1)
                    if hi == 4:
                        mm.then_inc(ring_done, 1)

                def level(j):
                    pe.wait_ge(lev_ready, 9 * n + j + 1)
                    for h in range(HEADS):
                        cols = slice(h * P, (h + 1) * P)
                        if j == 0:
                            for t in range(NT):
                                ts = slice(t * P, (t + 1) * P)
                                pe.matmul(ps[:, 4 + t, cols], KF[:, h, ts], Q[:, h, ts], start=True, stop=False)
                                mm = pe.matmul(ps[:, 4 + t, cols], KB[:, h, ts], Q[:, h, ts], start=False, stop=True)
                        elif j < 8:
                            for t in range(NT):
                                ts = slice(t * P, (t + 1) * P)
                                pe.matmul(ps[:, 4 + t, cols], KF[:, h, ts], QF[:, h, ts], start=True, stop=True)
                                mm = pe.matmul(ps[:, 6 + t, cols], KB[:, h, ts], QB[:, h, ts], start=True, stop=True)
                        else:
                            pe.matmul(ps[:, 4, cols], KF[:, h, 0:P], QF[:, h, P:T], start=True, stop=True)
                            mm = pe.matmul(ps[:, 5, cols], KB[:, h, P:T], QB[:, h, 0:P], start=True, stop=True)
                    mm.then_inc(lev_mm, 1)

                for c in range(3):
                    part(c, 0, 4)
                if m != 2:
                    for c in range(3, 8):
                        part(c, 0, 2)
                        level(2 * (c - 3))
                        part(c, 2, 4)
                        if c < 7:
                            level(2 * (c - 3) + 1)
                pe.wait_ge(scan_ready, m + 1)
                if m != 2:
                    for h in range(HEADS):
                        o = ps[:, 4 + h // 2, (h % 2) * T:(h % 2 + 1) * T]
                        for st in range(NT):
                            mm = pe.matmul(o, ivN[:, st, h * P:(h + 1) * P], att[:, st, h, :], start=st == 0,
                                           stop=m == 0 and st == NT - 1)
                        if m != 0:
                            if h == 0:
                                pe.wait_ge(st_out, 1 if m == 1 else 2)
                            pe.matmul(o, states[:, 0, h, :], QF[:, h, :], start=False, stop=False)
                            mm = pe.matmul(o, states[:, 1, h, :], QB[:, h, :], start=False, stop=True)
                    mm.then_inc(o_done, 1)
                    pe.wait_ge(o_sq, n + 1)
                    osq = OSQ.rearrange("p h t -> p (h t)")
                    for j in range(2):
                        mm = pe.matmul(ps[:, 6 + j, :], mean_mat[:, :], osq[:, j * 512:(j + 1) * 512], start=True, stop=True)
                    mm.then_inc(o_ms, 1)
                if m in (0, 2):
                    if m == 0:
                        pe.wait_ge(mix_ready, 1)
                    k = m // 2
                    for d, src in enumerate((KF, KB)):
                        for st in range(NT):
                            for h in range(HEADS):
                                mm = pe.transpose(ps[:, 4 + 2 * d + st, h * P:(h + 1) * P],
                                                  src[:, h, st * P:(st + 1) * P], ident[:, :])
                    mm.then_inc(kr_turned, 1)
                    pe.wait_ge(kr_out, k + 1)
                    for d in range(2):
                        for h in range(HEADS):
                            for st in range(NT):
                                mm = pe.matmul(ps[:, 4 + d, h * P:(h + 1) * P], KRN[:, d, st, h, :],
                                               ivN[:, st, h * P:(h + 1) * P], start=st == 0, stop=st == NT - 1)
                    mm.then_inc(st_done, 1)
                if m != 2:
                    pe.wait_ge(mix_ready, n + 1)
                    tokens(L_out[m], mixT)

            def peer(p):
                features(L_wq[p], hT)
                pe.wait_ge(bank_free, L_wq[p].e0 + 4 + 2)
                pe.wait_ge(subk_in, 16 * (p + 1))
                for t in range(NT):
                    if t:
                        pe.wait_ge(score_out, NT * p + t)
                    for j in range(2 * PH):
                        mm = pe.matmul(ps[:, 4 + j // 4, (j % 4) * P:(j % 4 + 1) * P], qrT[:, j, t * P:(t + 1) * P],
                                       subk[:, j, :], start=True, stop=True)
                    mm.then_inc(score_mm, 1)

            def attention():
                for j in range(NT * AH):
                    h, t = j // NT, j % NT
                    b, par = 4 + 2 * (j % 2), j % 2
                    if j >= 2:
                        pe.wait_ge(s_exp, 2 * (j - 1))
                    for half in range(2):
                        ds_ = slice(half * AD, (half + 1) * AD)
                        mm = pe.matmul(ps[:, b + half, :], qT[ds_, h, t * P:(t + 1) * P], kT[ds_, h, :], start=True, stop=True)
                    mm.then_inc(s_mm, 1)
                    if j >= 1:
                        attention_out(j - 1)
                attention_out(NT * AH - 1)

            def attention_out(j):
                h, par = j // NT, j % 2
                pe.wait_ge(a_ready, j + 1)
                for kt in range(4):
                    mm = pe.transpose(ps[:, par, kt * P:(kt + 1) * P], prob[:, par, 0, kt * P:(kt + 1) * P], ident[:, :])
                mm.then_inc(a_turned, 1)
                pe.wait_ge(a_out, j + 1)
                if j >= 2:
                    pe.wait_ge(ao_norm, j - 1)
                for kt in range(4):
                    mm = pe.matmul(ps[:, 2 + par, 0:P], aT[:, par, kt, :], vN[:, kt, h * P:(h + 1) * P],
                                   start=kt == 0, stop=kt == 3)
                mm.then_inc(ao_mm, 1)

            def mlp(i):
                turn_norm(f"n_m{i}")
                features(L_up[i], hT)
                L = L_down[i]
                for c in range(8):
                    e = L.e0 + c // 4
                    s = enter(L, c, 0, e if c % 4 == 0 else None)
                    pe.wait_ge(hid, 8 * i + min(2 * (c % 4) + 2, 8))
                    tokens_chunk(s, e, hidT, KT * (c % 4), c % 4 == 0, c % 4 == 3)

            pe.wait_ge(cond_ready, 1)
            modulation(0)
            for j, name in enumerate(("c0", "x0")):
                turn_norm("n_" + name)
                mixer(j)
                turn_norm("p_" + name)
                peer(j)
                modulation(j + 1)
            turn_norm("n_c1")
            mixer(2)
            turn_norm("n_x1")
            mixer(3)
            turn_norm("p_x1")
            peer(2)
            modulation(3)
            turn_norm("n_kv")
            tokens(L_kv, hT)
            turn("kc", kcN, bank_free, lambda t: L_kv.e0 + 2 + 2)
            wall_at(pe, 0)
            turn_norm("n_q")
            tokens(L_qkv, hT)
            turn("q", qN, heads_in, lambda t: t + 1)
            turn("kx", kxN, heads_in, lambda t: NT + t + 1)
            pe.wait_ge(tr_out, 4 * (turn_no["kx"] + 1))
            attention()
            turn("ao", oN, ao_norm, lambda t: NT * AH + t + 1)
            pe.wait_ge(tr_out, 4 * (turn_no["ao"] + 1))
            tokens(L_ao, hT)
            wall_at(pe, 1)
            mlp(0)
            wall_at(pe, 2)
            pe.wait_ge(tab_in, 16 * (N_ATT_TABS + N_HY_TABS))
            for j in range(3):
                if j:
                    pe.wait_ge(f_sin, j)
                n_in = EMB if j == 0 else ORDER
                pe.matmul(ps[0:ORDER, 4, 0:T], f_w[0:n_in, j, :], (f_emb if j == 0 else f_hid)[0:n_in, :],
                          start=True, stop=True).then_inc(f_mm, 1)
            pe.wait_ge(f_sin, 3)
            for t in range(NT):
                if t:
                    pe.wait_ge(f_taps, 1)
                for c in range(4):
                    mm = pe.matmul(ps[:, 4 + c, :], f_hid[0:ORDER, t * P:(t + 1) * P], f_out[0:ORDER, c * 512:(c + 1) * 512],
                                   start=True, stop=True)
                mm.then_inc(f_h, 1)

            def spectrum(srcs, n):
                for part in range(2):
                    if n or part:
                        pe.wait_ge(k_out, 2 * n + part)
                    for ft in range(NT):
                        for c in range(2):
                            for tt in range(NT):
                                mm = pe.matmul(ps[:, 4 + 2 * ft + c, :], dft[:, part, tt, ft * P:(ft + 1) * P],
                                               srcs[part](tt, c), start=tt == 0, stop=tt == NT - 1)
                    mm.then_inc(k_mm, 1)

            pe.wait_ge(f_pm, 1)
            spectrum([lambda tt, c: taps[:, tt, c * 512:(c + 1) * 512],
                      lambda tt, c: taps[:, tt, D + c * 512:D + (c + 1) * 512]], 0)
            wall_at(pe, 3)
            turn_norm("n_h")
            features(L_hin, hT)
            r = turn_no["vv"]
            pe.wait_ge(vv_ready, 1)
            for t in range(NT):
                for half in range(2):
                    for j in range(4):
                        mm = pe.transpose(ps[:, 4 + 2 * t + half, j * P:(j + 1) * P],
                                          zc[:, 16 + 4 * half + j, t * P:(t + 1) * P], ident[:, :])
                    mm.then_inc(tr_done, 1)
            pe.wait_ge(tr_out, 4 * (r + 1))
            spectrum([lambda tt, c: vNat[:, tt, c * 512:(c + 1) * 512]] * 2, 1)
            pe.wait_ge(y_freq, 1)
            for b in range(KT):
                o = ps[:, 4 + b // 2, (b % 2) * T:(b % 2 + 1) * T]
                for part in range(2):
                    for ft in range(NT):
                        mm = pe.matmul(o, Yf[:, part, ft, b * P:(b + 1) * P], idft[:, part, ft, :],
                                       start=part == 0 and ft == 0, stop=part == 1 and ft == NT - 1)
            mm.then_inc(conv_mm, 1)
            pe.wait_ge(vv_ready, 2)
            tokens(L_hout, hT)
            wall_at(pe, 4)
            mlp(1)
            wall_at(pe, 5)

        @block.scalar
        def _(act):
            st = Steps(act, act_step)
            roots = [0]

            def root(col):
                roots[0] += 1
                act.wait_ge(ms_ready, roots[0])
                act.activation(stat[:, col:col + NT], stat[:, col:col + NT], ACT.Sqrt, bias=eps[:, 0:1]).then_inc(root_ready, 1)

            def turn_norm(name):
                root(0)
                turn(name, hT)
            act.sem_inc(bank_free, 2)
            for s in range(2):
                act.sem_inc(mod_stored[s], 16)
            act.wait_ge(consts_in, 16 * N_CONSTS)
            act.activation(condS[:, :, :], condS[:, :, :], ACT.Silu).then_inc(cond_ready, 1)

            def pair(e):
                return ps[:, 2 * (e % 2):2 * (e % 2) + 2, :].rearrange("p a b -> p (a b)")

            def chunk_there(L, c):
                act.wait_ge(ring_done, L.g0 + c + 3)

            def copy_features(L, c, dst, func=ACT.Copy):
                chunk_there(L, c)
                act.activation(dst.rearrange("p b t -> p (b t)"), pair(L.e0 + c), func).then_inc(bank_free, 1)

            def copy_tokens(L, c, dst):
                chunk_there(L, c)
                e = L.e0 + c
                act.activation(dst, ps[:, 2 * (e % 2):2 * (e % 2) + 2, :], ACT.Copy).then_inc(bank_free, 1)

            def turn(name, dst):
                r = turn_no[name]
                for q in range(4):
                    t, half = q // 2, q % 2
                    act.wait_ge(tr_done, 4 * r + q + 1)
                    act.activation(dst[:, 4 * half:4 * half + 4, t * P:(t + 1) * P],
                                   ps[:, 4 + q, :].rearrange("p (j t) -> p j t", j=4), ACT.Copy).then_inc(tr_out, 1)


            def norm_pieces(name):
                root(0)
                yield
                turn(name, hT)
                yield

            def modulation(l):
                L = L_mod[l]
                for c in range(L.n):
                    s = c % 2
                    act.wait_ge(bank_free, L.e0 + c + 3)
                    act.dma_start(mods[l, :, c * CW:(c + 1) * CW], mod_io[0:2, s, :]).then_inc(mod_stored[s], 16)
                    yield

            def mixer(m):
                L = L_in[m]
                for c, s, k in ((0, SF, KF), (1, SB, KB)):
                    chunk_there(L, c)
                    act.activation(s.rearrange("p h t -> p (h t)"), pair(L.e0 + c), ACT.Sigmoid)
                    act.activation(k.rearrange("p h t -> p (h t)"), pair(L.e0 + c), ACT.Sigmoid,
                                   scale=-1.0).then_inc(bank_free, 1)
                    yield
                if m == 2:
                    copy_tokens(L, 2, ivN)
                    yield
                else:
                    n = {0: 0, 1: 1, 3: 2}[m]
                    copy_features(L, 2, Q)
                    yield
                    copy_tokens(L, 3, ivN)
                    yield
                    yield
                    for c, dst, func in ((4, CG, ACT.Copy), (5, HV, ACT.Copy), (6, BG, ACT.Copy), (7, G, ACT.Silu)):
                        copy_features(L, c, dst, func)
                        yield
                        if c < 7:
                            yield
                    act.wait_ge(o_done, n + 1)
                    act.activation(OSQ.rearrange("p h t -> p (h t)"), ps[:, 4:6, :].rearrange("p a b -> p (a b)"),
                                   ACT.Square).then_inc(o_sq, 1)
                    yield
                    act.wait_ge(o_ms, n + 1)
                    act.activation(ORS.rearrange("p h t -> p (h t)"), ps[:, 6:8, :].rearrange("p a b -> p (a b)"),
                                   ACT.Sqrt, bias=eps[:, 0:1]).then_inc(o_root, 1)
                    yield
                if m in (0, 2):
                    k = m // 2
                    act.wait_ge(kr_turned, k + 1)
                    act.activation(KRN.rearrange("p d s h k -> p (d s) (h k)"), ps[:, 4:8, :], ACT.Copy).then_inc(kr_out, 1)
                    yield
                    act.wait_ge(st_done, k + 1)
                    act.activation(states[:, :, :, :].rearrange("p d h v -> p d (h v)"), ps[:, 4:6, :],
                                   ACT.Copy).then_inc(st_out, 1)
                    yield
                if m != 2:
                    yield
                    yield

            def peer_queries(p):
                for c in range(4):
                    copy_features(L_wq[p], c, qrT[:, 4 * c:4 * c + 4, :])
                    yield

            def peer_part(p, n):
                t, q = n // PARTS, n % PARTS
                if q == 0:
                    act.wait_ge(score_mm, NT * p + t + 1)
                    if t:
                        act.wait_ge(picks, PARTS * (NT * p + t))
                    act.activation(sc.rearrange("p j k -> p (j k)"), ps[:, 4:8, :].rearrange("p a b -> p (a b)"),
                                   ACT.Copy).then_inc(score_out, 1)
                yield
                yield
                act.wait_ge(gate_sub, PARTS * NT * p + n + 1)
                h = slice(q * HQ, (q + 1) * HQ)
                act.activation(top[:, h, :], top[:, h, :], ACT.Exp).then_inc(gate_exp, 1)
                yield
                yield
                yield

            def peer_parts(p):
                return [peer_part(p, n) for n in range(1, NT * PARTS)]

            def gelu(K, u, i=0):
                s = slice((u % 2) * GROUP, (u % 2 + 1) * GROUP)
                act.wait_ge(dot_done, i * (2 * GROUP) + (GROUP * (K + u + 1) + GROUP))
                act.activation(coef[:, s], dots[:, s], ACT.Gelu).then_inc(gelu_done, 1)

            def segment(p, g):
                if g < ALLGRP:
                    gelu(ALLGRP * p, g)

            def segments(p, g, n):
                with act.Fori(0, n // 2) as i:
                    for u in range(2):
                        gelu(ALLGRP * p, g + u, i)

            def kv_pieces():
                for c, dst in enumerate((kcN[:, :, 0:CW], kcN[:, :, CW:D], vN[:, 0:NT, 0:CW], vN[:, 0:NT, CW:D])):
                    copy_tokens(L_kv, c, dst)
                    yield
                turn("kc", kT[:, :, 0:T])
                yield

            def attention():
                for j in range(NT * AH):
                    b, par = 4 + 2 * (j % 2), j % 2
                    act.wait_ge(s_bias, j + 1)
                    if j >= 2:
                        act.wait_ge(a_turned, j - 1)
                    for half in range(2):
                        act.activation(prob[:, par, half, :], ps[:, b + half, :], ACT.Exp, scale=AD ** -0.5,
                                       bias=a_small[:, par, half:half + 1],
                                       accum_out=a_small[:, par, 2 + half:3 + half]).then_inc(s_exp, 1)
                    if j >= 1:
                        attention_out(j - 1)
                attention_out(NT * AH - 1)
                act.wait_ge(ao_sq, NT * AH)
                act.activation(ao_ms, ao_ms, ACT.Sqrt, scale=1.0 / P, bias=eps[:, 0:1]).then_inc(ao_root, 1)

            def attention_out(j):
                par = j % 2
                act.wait_ge(a_turned, j + 1)
                if j >= 2:
                    act.wait_ge(ao_mm, j - 1)
                act.activation(aT[:, par].rearrange("p a b -> p (a b)"), ps[:, par, :], ACT.Copy).then_inc(a_out, 1)
                act.wait_ge(ao_mm, j + 1)
                act.activation(rope_tmp[:, par * P:(par + 1) * P], ps[:, 2 + par, 0:P], ACT.Square,
                               accum_out=ao_ms[:, j:j + 1]).then_inc(ao_sq, 1)

            def mlp(i):
                turn_norm(f"n_m{i}")
                L = L_up[i]
                for c in range(8):
                    h = hidT[:, 4 * c:4 * c + 4, :]
                    copy_features(L, c, h, ACT.Relu)
                    act.wait_ge(bank_free, L.e0 + c + 3)
                    act.activation(h, h, ACT.Square).then_inc(hid, 1)
                L = L_down[i]
                for c in range(2):
                    act.wait_ge(ring_done, L.g0 + 4 * c + 3 + 3)
                    e = L.e0 + c
                    act.activation(yM[:, :, c * CW:(c + 1) * CW], ps[:, 2 * (e % 2):2 * (e % 2) + 2, :],
                                   ACT.Copy).then_inc(bank_free, 1)
                root(2)

            act.wait_ge(lam_sums, 1)
            act.activation(lb[:, :, :, :], lb[:, :, :, :], ACT.Exp).then_inc(lam_exps, 1)
            run(modulation(0))
            run(norm_pieces("n_c0"), mixer(0), norm_pieces("p_c0"), peer_queries(0), peer_part(0, 0))
            weave(0, RATE[0], segment, segments, blend(peer_parts(0), modulation(1)), norm_pieces("n_x0"), mixer(1), norm_pieces("p_x0"),
                  peer_queries(1), peer_part(1, 0))
            weave(1, RATE[1], segment, segments, blend(peer_parts(1), modulation(2)), norm_pieces("n_c1"), mixer(2))
            run(norm_pieces("n_x1"), mixer(3), norm_pieces("p_x1"), peer_queries(2), peer_part(2, 0))
            weave(2, RATE[2], segment, segments, blend(peer_parts(2), modulation(3)), norm_pieces("n_kv"), kv_pieces())
            root(0)
            wall_at(act, 0)
            turn_norm("n_q")
            for c, dst in enumerate((qN[:, :, 0:CW], qN[:, :, CW:D], kxN[:, :, 0:CW], kxN[:, :, CW:D],
                                     vN[:, NT:, 0:CW], vN[:, NT:, CW:D])):
                copy_tokens(L_qkv, c, dst)
            act.wait_ge(lam_sums, 2)
            act.activation(stat[:, 8:10], stat[:, 8:10], ACT.Exp).then_inc(lam_exps, 1)
            turn("q", qT)
            turn("kx", kT[:, :, T:2 * T])
            attention()
            turn("ao", hT)
            for c in range(2):
                copy_tokens(L_ao, c, yA[:, :, c * CW:(c + 1) * CW])
            root(2)
            wall_at(act, 1)
            mlp(0)
            wall_at(act, 2)
            act.wait_ge(tab_in, 16 * (N_ATT_TABS + N_HY_TABS))
            act.wait_ge(f_arg, 1)
            for j in range(3):
                act.wait_ge(f_mm, j + 1)
                act.activation(f_x[0:ORDER, :], ps[0:ORDER, 4, 0:T], ACT.Identity, scale=f_b[0:ORDER, 3:4],
                               bias=f_b[0:ORDER, 4 + j:5 + j]).then_inc(f_lin, 1)
                act.wait_ge(f_red, j + 1)
                act.activation(f_hid[0:ORDER, :], f_x[0:ORDER, :], ACT.Sin).then_inc(f_sin, 1)

            def spectrum(dst, n):
                for part in range(2):
                    act.wait_ge(k_mm, 2 * n + part + 1)
                    act.activation(dst[:, part].rearrange("p t (c d) -> p (t c) d", c=2), ps[:, 4:8, :],
                                   ACT.Copy).then_inc(k_out, 1)

            spectrum(Kf, 0)
            wall_at(act, 3)
            turn_norm("n_h")
            for c in range(6):
                chunk_there(L_hin, c)
                e = L_hin.e0 + c
                for b in range(4):
                    j = 4 * c + b
                    ins = act.activation(zT[:, j, :], ps[:, 2 * (e % 2) + b // 2, (b % 2) * T:(b % 2 + 1) * T],
                                         ACT.Identity, bias=hyb[:, j:j + 1])
                ins.then_inc(bank_free, 1)
            r = turn_no["vv"]
            for q in range(4):
                act.wait_ge(tr_done, 4 * r + q + 1)
                act.activation(vNat[:, q // 2, (q % 2) * 512:(q % 2 + 1) * 512], ps[:, 4 + q, :], ACT.Copy).then_inc(tr_out, 1)
            spectrum(Vf, 1)
            root(2)
            wall_at(act, 4)
            mlp(1)
            wall_at(act, 5)

        @block.vector
        def _(dve):
            st = Steps(dve, dve_step)
            roots = [0]
            dve.sem_inc(axpy_done, 2 * GROUP)
            dve.sem_inc(dot_done, GROUP)
            dve.wait_ge(consts_in, 16 * N_CONSTS)
            st.do(dve.tensor_copy(masks[:, :, :], mask_f))
            st.do(dve.tensor_tensor(oml[:, 0], lb[:, 0], lb[:, 1], ALU.max))
            st.settle()
            st.do(dve.tensor_tensor(lb[:, 0], lb[:, 0], oml[:, 0], ALU.subtract))
            dve.tensor_tensor(lb[:, 1], lb[:, 1], oml[:, 0], ALU.subtract).then_inc(lam_sums, 1)
            dve.wait_ge(lam_exps, 1)
            st.do(dve.tensor_tensor(oml[:, 0], lb[:, 0], lb[:, 1], ALU.add))
            st.settle()
            st.do(dve.reciprocal(oml[:, 1], oml[:, 0]))
            st.settle()
            st.do(dve.tensor_tensor(lb[:, 0], lb[:, 0], oml[:, 1], ALU.mult))
            st.do(dve.tensor_tensor(lb[:, 1], lb[:, 1], oml[:, 1], ALU.mult))
            st.settle()
            st.do(dve.tensor_tensor(lb[:, 1], lb[:, 0], lb[:, 1], ALU.add))
            st.settle()
            st.do(dve.tensor_tensor(lb[:, 1], lb[:, 1], lb[:, 0], ALU.subtract))
            st.settle()
            st.do(dve.tensor_tensor(lb[:, 0], lb[:, 0], lb[:, 0], ALU.subtract))
            st.settle()
            st.do(dve.tensor_scalar(oml[:, :], lb[:, :], -1.0, 1.0, ALU.mult, ALU.add))
            def rms(src, col, junk):
                for t in range(NT):
                    ins = dve.tensor_tensor_reduce(junk[:, t, :], src[:, t, :], src[:, t, :], 1.0 / D, 0.0, ALU.mult,
                                                   ALU.add, stat[:, col + t:col + t + 1])
                ins.then_inc(ms_ready, 1)
                roots[0] += 1
                dve.wait_ge(root_ready, roots[0])
                st.do(dve.reciprocal(stat[:, col:col + NT], stat[:, col:col + NT]))
                st.settle()

            def norm(name, src):
                hN = norm_buf[name]
                rms(src, 0, hN)
                dve.wait_ge(vec_full, rows_in[name])
                st.do(dve.scalar_tensor_tensor(vec[:, SCALE, :], vec[:, SCALE, :], 1.0, vec[:, GAIN, :], ALU.add, ALU.mult))
                st.settle()
                for t in range(NT):
                    st.do(dve.scalar_tensor_tensor(hN[:, t, :], src[:, t, :], stat[:, t:t + 1], vec[:, SCALE, :],
                                                   ALU.mult, ALU.mult))
                st.settle()
                for t in range(NT):
                    dve.tensor_tensor(hN[:, t, :], hN[:, t, :], vec[:, SHIFT, :], ALU.add).then_inc(normed, 1)
                dve.wait_ge(normed, NT * (norm_no[name] + 1))
                dve.sem_inc(vec_used, 1)

            def norm_pieces(name, src):
                norm(name, src)
                yield
                yield

            def gated(name, L, dst, tmp):
                dve.wait_ge(vec_full, rows_in[name])
                for c in range(2):
                    cols = slice(c * CW, (c + 1) * CW)
                    e = L.e0 + c
                    dve.wait_ge(ring_done, L.g0 + c + 3)
                    st.do(dve.tensor_tensor(tmp[:, 0, cols], ps[:, 2 * (e % 2), :], vec[:, GATE, cols], ALU.mult))
                    dve.tensor_tensor(tmp[:, 1, cols], ps[:, 2 * (e % 2) + 1, :], vec[:, GATE, cols],
                                      ALU.mult).then_inc(bank_free, 1)
                    if c == 0:
                        yield
                dve.wait_ge(bank_free, L.e0 + 2 + 2)
                for t in range(NT):
                    ins = dve.tensor_tensor(dst[:, t, :], dst[:, t, :], tmp[:, t, :], ALU.add)
                    if t < NT - 1:
                        st.do(ins)
                ins.then_inc(resid, 1)
                dve.wait_ge(resid, resid_no[name] + 1)
                dve.sem_inc(vec_used, 1)
                yield

            def post(name, y):
                dve.wait_ge(vec_full, rows_in[name])
                rms(y, 2, hA)
                st.do(dve.tensor_tensor(vec[:, GAIN, :], vec[:, GAIN, :], vec[:, GATE, :], ALU.mult))
                st.settle()
                for t in range(NT):
                    st.do(dve.scalar_tensor_tensor(hA[:, t, :], y[:, t, :], stat[:, 2 + t:3 + t], vec[:, GAIN, :],
                                                   ALU.mult, ALU.mult))
                st.settle()
                for t in range(NT):
                    ins = dve.tensor_tensor(xs[:, t, :], xs[:, t, :], hA[:, t, :], ALU.add)
                    if t < NT - 1:
                        st.do(ins)
                ins.then_inc(resid, 1)
                dve.wait_ge(resid, resid_no[name] + 1)
                dve.sem_inc(vec_used, 1)

            def flat(b):
                return b.rearrange("p h t -> p (h t)")

            def scan_update(l, queries, last):
                B = 1 << l

                def halves(b):
                    v = flat(b).rearrange("p (n two b) -> p n two b", two=2, b=B)
                    return v[:, :, 0, :], v[:, :, 1, :]

                n = HEADS * T // (2 * B)

                def spread(d, side):
                    return halves((SF, SB)[d])[side][:, :, 0:1].to_broadcast([P, n, B])

                todo = []
                if queries:
                    todo += [(halves(QF)[1], spread(0, 0)), (halves(QB)[0], spread(1, 1))]
                todo += [(halves(KF)[0], spread(0, 1)), (halves(KB)[1], spread(1, 0))]
                for j, (b, f) in enumerate(todo):
                    st.do(dve.tensor_tensor(b, b, f, ALU.mult))
                st.settle()
                for d in range(2):
                    left, right = [v[:, :, 0] for v in halves((SF, SB)[d])]
                    ins = dve.tensor_tensor(left, left, right, ALU.mult)
                    if d == 0:
                        st.do(ins)
                last(ins)

            def mixer(m):
                L = L_in[m]
                l = 0 if m < 2 else 1
                for d, (s, k) in enumerate(((SF, KF), (SB, KB))):
                    if m == 2 or d == 0:
                        yield
                    dve.wait_ge(bank_free, L.e0 + d + 3)
                    for h in range(HEADS):
                        o1, l1 = oml[:, l, d, h:h + 1], lb[:, l, d, h:h + 1]
                        st.do(dve.tensor_scalar(s[:, h, :], s[:, h, :], o1, l1, ALU.mult, ALU.add))
                        st.do(dve.tensor_scalar(k[:, h, :], k[:, h, :], o1, None, ALU.mult))
                st.settle()
                st.do(dve.tensor_scalar(flat(SF), flat(SF), FLOOR, None, ALU.max))
                st.do(dve.tensor_scalar(flat(SB), flat(SB), FLOOR, None, ALU.max))
                st.settle()
                if m == 2:
                    yield
                    for lev in range(LEVELS):
                        if lev < LEVELS - 1:
                            scan_update(lev, False, st.do)
                            st.settle()
                        else:
                            scan_update(lev, False, lambda ins: ins.then_inc(scan_ready, 1))
                    yield
                    yield
                    return
                n = {0: 0, 1: 1, 3: 2}[m]
                yield
                dve.wait_ge(bank_free, L.e0 + 2 + 3)
                st.do(dve.tensor_tensor(flat(QF), flat(Q), flat(SF), ALU.mult))
                dve.tensor_tensor(flat(QB), flat(Q), flat(SB), ALU.mult).then_inc(lev_ready, 1)
                dve.wait_ge(lev_ready, 9 * n + 1)
                yield
                dve.wait_ge(lev_mm, 9 * n + 1)
                for t in range(NT):
                    ins = dve.tensor_tensor(att[:, t, :, t * P:(t + 1) * P],
                                            ps[:, 4 + t, :].rearrange("p (h t) -> p h t", h=HEADS),
                                            ident[:, :].unsqueeze(1).to_broadcast([P, HEADS, P]), ALU.mult)
                    if t < NT - 1:
                        st.do(ins)
                ins.then_inc(lev_ready, 1)
                yield
                for j in range(1, 8):
                    lev = j - 1
                    dve.wait_ge(lev_mm, 9 * n + j + 1)
                    for d in range(2):
                        for t in range(NT):
                            st.do(dve.copy_predicated(
                                att[:, t, :, t * P:(t + 1) * P],
                                masks[:, 7 * d + lev, :].unsqueeze(1).to_broadcast([P, HEADS, P]),
                                ps[:, 4 + 2 * d + t, :].rearrange("p (h t) -> p h t", h=HEADS)))
                        st.settle()
                    scan_update(lev, True, lambda ins: ins.then_inc(lev_ready, 1))
                    dve.wait_ge(lev_ready, 9 * n + j + 2)
                    yield
                dve.wait_ge(lev_mm, 9 * n + 9)
                for st_, b in ((0, 4), (1, 5)):
                    o = slice((1 - st_) * P, (2 - st_) * P)
                    st.do(dve.tensor_copy(att[:, st_, :, o], ps[:, b, :].rearrange("p (h t) -> p h t", h=HEADS)))
                scan_update(LEVELS - 1, True, lambda ins: ins.then_inc(scan_ready, 1))
                yield

                dve.wait_ge(bank_free, L.e0 + 7 + 3)
                CU = CG
                st.do(dve.tensor_tensor(flat(CU), flat(CG), flat(HV), ALU.mult))
                st.settle()
                for b in range(HEADS):
                    st.do(dve.tensor_scalar(mixT[:, 4 + b, :], CU[:, b, :], convc[:, l, b, 1:2], None, ALU.mult))
                st.settle()
                for tap, sign in ((0, -1), (2, 1)):
                    for b in range(HEADS):
                        w = convc[:, l, b, tap:tap + 1]
                        y, u = mixT[:, 4 + b, :], CU[:, b, :]
                        if m == 0:
                            y, u, hop, size = y.unsqueeze(1), u.unsqueeze(1), 1, T
                        elif b < 2:
                            y, u = [v.rearrange("p (r c) -> p r c", c=GRID_W) for v in (y, u)]
                            hop, size = 1, GRID_W
                        else:
                            y, u, hop, size = y.unsqueeze(1), u.unsqueeze(1), GRID_W, T
                        to = slice(hop, size) if sign < 0 else slice(0, size - hop)
                        fr = slice(0, size - hop) if sign < 0 else slice(hop, size)
                        st.do(dve.scalar_tensor_tensor(y[:, :, to], u[:, :, fr], w, y[:, :, to], ALU.mult, ALU.add))
                    st.settle()
                st.do(dve.tensor_tensor(mixT[:, 4:8, :], mixT[:, 4:8, :], BG, ALU.mult))

                yield
                dve.wait_ge(o_root, n + 1)
                st.do(dve.reciprocal(flat(ORS), flat(ORS)))
                st.settle()
                st.do(dve.tensor_tensor(flat(ORS), flat(ORS), flat(G), ALU.mult))
                st.settle()
                dve.tensor_tensor(mixT[:, 0:4, :].rearrange("p h t -> p (h t)"),
                                  ps[:, 4:6, :].rearrange("p a b -> p (a b)"), flat(ORS), ALU.mult).then_inc(mix_ready, 1)
                yield
                if m == 0:
                    yield
                    yield
                name, dst, tmp = (("r_c0", cs, hA), ("r_x0", xs, hB), None, ("r_x1", xs, hA))[m]
                yield from gated(name, L_out[m], dst, tmp)

            def top16(values, index, source, rows_):
                for j in rows_:
                    st.do(dve.max(values(j)[:, 0:8], source(j)))
                st.settle()
                for j in rows_:
                    st.do(dve.max_index(index(j)[:, 0:8], values(j)[:, 0:8], source(j)))
                st.settle()
                for j in rows_:
                    st.do(dve.match_replace(source(j), values(j)[:, 0:8], source(j), NEG))
                st.settle()
                for j in rows_:
                    st.do(dve.max(values(j)[:, 8:16], source(j)))
                st.settle()
                for j in rows_:
                    st.do(dve.max_index(index(j)[:, 8:16], values(j)[:, 8:16], source(j)))
                st.settle()

            def peer_queries(p):
                for _ in range(4):
                    yield

            def peer_part(p, n):
                l, par, t, q = p // 2, p % 2, n // PARTS, n % PARTS
                h = slice(q * HQ, (q + 1) * HQ)
                r = slice(q * NQ, (q + 1) * NQ)
                if q == 0:
                    dve.wait_ge(score_out, NT * p + t + 1)
                top16(lambda j: vals[:, j // 2, j % 2, :], lambda j: vidx[:, j // 2, j % 2, :],
                      lambda j: sc[:, j, :], range(2 * q * HQ, 2 * (q + 1) * HQ))
                yield
                st.do(dve.tensor_copy(vidx_f[:, h], vidx[:, h]))
                st.do(dve.tensor_tensor(cand[:, h], vals[:, h, 0, :].unsqueeze(3).to_broadcast([P, HQ, TOPK, TOPK]),
                                        vals[:, h, 1, :].unsqueeze(2).to_broadcast([P, HQ, TOPK, TOPK]), ALU.add))
                st.settle()
                candr = cand.rearrange("p h a b -> p h (a b)")
                top16(lambda j: top[:, j, :], lambda j: pos[:, j, :], lambda j: candr[:, j, :], range(q * HQ, (q + 1) * HQ))
                yield
                z = zsum[:, h].unsqueeze(2).to_broadcast([P, HQ, TOPK])
                st.do(dve.tensor_copy(zsum[:, h], top[:, h, 0]))
                st.settle()
                dve.tensor_tensor(top[:, h], top[:, h], z, ALU.subtract).then_inc(gate_sub, 1)
                posr = pos.rearrange("p h k -> p (h k)")[:, r]
                st.do(dve.tensor_scalar(pos2[:, 0, r], posr, 4, None, ALU.logical_shift_right))
                st.do(dve.tensor_scalar(pos2[:, 1, r], posr, TOPK - 1, None, ALU.bitwise_and))
                st.settle()
                st.do(dve.tensor_copy(pos_f[:, :, r], pos2[:, :, r]))
                st.settle()
                eq = eqs[:, r, :]
                eq4 = eq.rearrange("p (h k) a -> p h k a", h=HQ)
                for half in range(2):
                    st.do(dve.tensor_tensor(eq, pos_f[:, half, r].unsqueeze(2).to_broadcast([P, NQ, TOPK]),
                                            iota16[:, :].unsqueeze(1).to_broadcast([P, NQ, TOPK]), ALU.is_equal))
                    st.settle()
                    st.do(dve.tensor_tensor(eq4, eq4, vidx_f[:, h, half, :].unsqueeze(2).to_broadcast([P, HQ, TOPK, TOPK]),
                                            ALU.mult))
                    st.settle()
                    st.do(dve.reduce_sum(sel[:, half, r], eq, AX))
                    st.settle()
                    yield
                st.do(dve.tensor_scalar(eidx_f[:, r], sel[:, 0, r], float(PK), float(l * NEXP), ALU.mult, ALU.add))
                st.settle()
                st.do(dve.tensor_tensor(eidx_f[:, r], eidx_f[:, r], sel[:, 1, r], ALU.add))
                st.settle()
                st.do(dve.tensor_copy(eidx[:, par, t, r], eidx_f[:, r]))
                dve.wait_ge(gate_exp, PARTS * NT * p + n + 1)
                st.do(dve.reduce_sum(zsum[:, h], top[:, h], AX))
                st.settle()
                st.do(dve.reciprocal(zsum[:, h], zsum[:, h]))
                st.settle()
                dve.tensor_tensor(gates[:, par, t, r].rearrange("p (h k) -> p h k", h=HQ), top[:, h], z, ALU.mult).then_inc(picks, 1)
                dve.wait_ge(picks, PARTS * NT * p + n + 1)
                yield

            def peer_parts(p):
                return [peer_part(p, n) for n in range(1, NT * PARTS)]

            peer_buf, peer_dst = (hA, hB, hA), (cs, xs, xs)

            def dot(p, t, K, u, s, i):
                col = (u % 2) * GROUP + s
                dve.wait_ge(u_full[s], i * 32 + 16 * (K + u + 1))
                dve.tensor_tensor_reduce(ubuf[:, s, :], ubuf[:, s, :], peer_buf[p][:, t, :], 1.0, 0.0, ALU.mult,
                                         ALU.add, dots[:, col:col + 1]).then_inc(dot_done, 1)

            def weigh(p, t, K, u, i):
                grp = slice((u % 2) * GROUP, (u % 2 + 1) * GROUP)
                dve.wait_ge(gelu_done, i * 2 + (K + u + 1))
                g0 = (u % NGRP) * GROUP
                col = slice(g0, g0 + GROUP) if isinstance(i, int) else bass.ds(i * (2 * GROUP) + g0, GROUP)
                dve.tensor_tensor(coef[:, grp], coef[:, grp], gates[:, p % 2, t, col], ALU.mult).then_inc(coef_ready, 1)

            def add_row(K, u, s, i):
                v = (u % 2) * GROUP + s
                if s == 0:
                    dve.wait_ge(coef_ready, i * 2 + (K + u + 1))
                dve.wait_ge(v_full[v], i * 16 + 16 * ((K + u) // 2 + 1))
                dve.wait_ge(axpy_done, i * (2 * GROUP) + (GROUP * (K + u) + s + 2 * GROUP))
                c = coef[:, v:v + 1]
                if u % NGRP == 0 and s == 0:
                    ins = dve.tensor_scalar(acc, vbuf[:, v, :], c, None, ALU.mult)
                else:
                    ins = dve.scalar_tensor_tensor(acc, vbuf[:, v, :], c, acc, ALU.mult, ALU.add)
                ins.then_inc(axpy_done, 1)

            def group(p, g, i=0):
                K = ALLGRP * p
                for s in range(GROUP):
                    if g < ALLGRP:
                        dot(p, g // NGRP, K, g, s, i)
                    if g > 0 and s == 0:
                        weigh(p, (g - 1) // NGRP, K, g - 1, i)
                    if g > 0 and s > 0:
                        add_row(K, g - 1, s - 1, i)
                if g > 0:
                    add_row(K, g - 1, GROUP - 1, i)

            def flush(p, t):
                dve.wait_ge(axpy_done, GROUP * (ALLGRP * p + NGRP * (t + 1)) + 2 * GROUP)
                if t == 0:
                    dve.wait_ge(pgate_in, 16 * (p + 1))
                st.do(dve.tensor_tensor(acc, acc, pgate[:, :], ALU.mult))
                st.settle()
                dst = peer_dst[p][:, t, :]
                ins = dve.tensor_tensor(dst, dst, acc, ALU.add)
                if t < NT - 1:
                    st.do(ins)
                    st.settle()
                else:
                    ins.then_inc(peer_out, 1)
                    dve.wait_ge(peer_out, p + 1)

            def segment(p, g):
                group(p, g)
                if g > 0 and g % NGRP == 0:
                    flush(p, g // NGRP - 1)

            def segments(p, g, n):
                with dve.Fori(0, n // 2) as i:
                    for u in range(2):
                        group(p, g + u, i)

            def modulation(l):
                L = L_mod[l]
                for c in range(L.n):
                    e, s = L.e0 + c, c % 2
                    dve.wait_ge(ring_done, L.g0 + c + 3)
                    dve.wait_ge(bias_in[s], 16 * (6 * l + c // 2 + 1))
                    dve.tensor_tensor(mod_io[0:2, s, :], mod_io[0:2, s, :], ps[0:2, 2 * (e % 2), :], ALU.add).then_inc(bank_free, 1)
                    yield

            def kv_pieces():
                for _ in range(5):
                    yield

            run(modulation(0))
            run(norm_pieces("n_c0", cs), mixer(0), norm_pieces("p_c0", cs), peer_queries(0), peer_part(0, 0))
            weave(0, RATE[0], segment, segments, blend(peer_parts(0), modulation(1)), norm_pieces("n_x0", xs), mixer(1), norm_pieces("p_x0", xs),
                  peer_queries(1), peer_part(1, 0))
            weave(1, RATE[1], segment, segments, blend(peer_parts(1), modulation(2)), norm_pieces("n_c1", cs), mixer(2))
            run(norm_pieces("n_x1", xs), mixer(3), norm_pieces("p_x1", xs), peer_queries(2), peer_part(2, 0))

            def context_pieces():
                dve.wait_ge(ctx2_in, 16)
                yield from norm_pieces("n_kv", cs)

            weave(2, RATE[2], segment, segments, blend(peer_parts(2), modulation(3)), context_pieces(), kv_pieces())
            rms(xs, 0, hA)
            dve.wait_ge(vec_full, rows_in["final"])
            for t in range(NT):
                ins = dve.scalar_tensor_tensor(xs[:, t, :], xs[:, t, :], stat[:, t:t + 1], vec[:, GAIN, :], ALU.mult, ALU.mult)
                if t < NT - 1:
                    st.do(ins)
            ins.then_inc(resid, 1)
            dve.wait_ge(resid, resid_no["final"] + 1)
            dve.sem_inc(vec_used, 1)
            wall_at(dve, 0)

            norm("n_q", xs)
            dve.wait_ge(tab_in, 16 * N_ATT_TABS)
            for j in range(2):
                ins = dve.tensor_tensor_reduce(lam_tmp[:, j, :], lam_in[:, 2 * j, :], lam_in[:, 2 * j + 1, :], 1.0, 0.0,
                                               ALU.mult, ALU.add, stat[:, 8 + j:9 + j])
                if j == 0:
                    st.do(ins)
            ins.then_inc(lam_sums, 1)
            st.do(dve.tensor_scalar(subln, subln, 1.0 - LAM_INIT, None, ALU.mult))
            for src, e in ((qN, L_qkv.e0 + 1), (kxN, L_qkv.e0 + 3)):
                dve.wait_ge(bank_free, e + 3)
                for t in range(NT):
                    v = src[:, t, :]
                    a4 = v.rearrange("p (h c x f) -> p h c x f", h=2 * AH, c=2, x=2)
                    o4 = rope_tmp.rearrange("p (h c x f) -> p h c x f", h=2 * AH, c=2, x=2)
                    for x in range(2):
                        st.do(dve.tensor_tensor(o4[:, :, :, x, :], a4[:, :, :, 1 - x, :],
                                                sinT[:, t, :, x, :].unsqueeze(1).to_broadcast([P, 2 * AH, 2, 16]), ALU.mult))
                    st.settle()
                    vh = v.rearrange("p (h d) -> p h d", d=AD)
                    st.do(dve.tensor_tensor(vh, vh, cosT[:, t, :].unsqueeze(1).to_broadcast([P, 2 * AH, AD]), ALU.mult))
                    st.settle()
                    dve.tensor_tensor(v, v, rope_tmp, ALU.add).then_inc(heads_in, 1)
                    dve.wait_ge(heads_in, (0 if src is qN else NT) + t + 1)
            dve.wait_ge(lam_exps, 2)
            st.do(dve.tensor_tensor(stat[:, 10:11], stat[:, 8:9], stat[:, 9:10], ALU.subtract))
            st.settle()
            st.do(dve.tensor_scalar(stat[:, 10:11], stat[:, 10:11], -1.0, -LAM_INIT, ALU.mult, ALU.add))
            st.settle()

            def attention_out(j):
                h, t, par = j // NT, j % NT, j % 2
                dve.wait_ge(ao_sq, j + 1)
                dve.tensor_tensor(oN[:, t, h * P:(h + 1) * P], ps[:, 2 + par, 0:P], subln, ALU.mult).then_inc(ao_norm, 1)

            for j in range(NT * AH):
                b, par = 4 + 2 * (j % 2), j % 2
                dve.wait_ge(s_mm, j + 1)
                st.do(dve.tensor_reduce(a_small[:, par, 0:2], ps[:, b:b + 2, :], AX, ALU.max))
                st.settle()
                dve.tensor_scalar(a_small[:, par, 0:2], a_small[:, par, 0:2], -AD ** -0.5, None, ALU.mult).then_inc(s_bias, 1)
                if j >= 1:
                    attention_out(j - 1)
                dve.wait_ge(s_exp, 2 * j + 2)
                st.do(dve.reciprocal(a_small[:, par, 2:4], a_small[:, par, 2:4]))
                st.settle()
                st.do(dve.tensor_scalar(a_small[:, par, 3:4], a_small[:, par, 3:4], stat[:, 10:11], None, ALU.mult))
                st.do(dve.tensor_scalar(prob[:, par, 0, :], prob[:, par, 0, :], a_small[:, par, 2:3], None, ALU.mult))
                st.settle()
                dve.scalar_tensor_tensor(prob[:, par, 0, :], prob[:, par, 1, :], a_small[:, par, 3:4], prob[:, par, 0, :],
                                         ALU.mult, ALU.add).then_inc(a_ready, 1)
            attention_out(NT * AH - 1)
            dve.wait_ge(ao_root, 1)
            st.do(dve.reciprocal(ao_ms, ao_ms))
            st.settle()
            dve.wait_ge(ao_norm, NT * AH)
            for t in range(NT):
                o = oN[:, t, :].rearrange("p (h d) -> p h d", h=AH)
                r = ao_ms.rearrange("p (h t) -> p t h", t=NT)[:, t, :].unsqueeze(2).to_broadcast([P, AH, P])
                dve.tensor_tensor(o, o, r, ALU.mult).then_inc(ao_norm, 1)
            dve.wait_ge(bank_free, L_ao.e0 + 2 + 2)
            post("o_0", yA)
            wall_at(dve, 1)

            def mlp(i):
                norm(f"n_m{i}", xs)
                dve.wait_ge(bank_free, L_down[i].e0 + 2 + 2)
                post(f"m_{i}", yM)

            mlp(0)
            wall_at(dve, 2)

            dve.wait_ge(tab_in, 16 * (N_ATT_TABS + N_HY_TABS))
            dve.tensor_scalar(f_b[0:ORDER, 4:7], f_b[0:ORDER, 0:3], f_b[0:ORDER, 3:4], None, ALU.mult).then_inc(f_arg, 1)
            hi = float(np.float32(TWO_PI))
            lo = float(np.float32(TWO_PI - np.float64(np.float32(TWO_PI))))
            fx, fn = f_x[0:ORDER, :], f_n[0:ORDER, :]
            for j in range(3):
                dve.wait_ge(f_lin, j + 1)
                st.do(dve.tensor_scalar(fn, fx, 1.0 / TWO_PI, ROUND, ALU.mult, ALU.add))
                st.settle()
                st.do(dve.tensor_scalar(fn, fn, ROUND, None, ALU.subtract))
                st.settle()
                st.do(dve.scalar_tensor_tensor(fx, fn, -hi, fx, ALU.mult, ALU.add))
                st.settle()
                st.do(dve.scalar_tensor_tensor(fx, fn, -lo, fx, ALU.mult, ALU.add))
                st.settle()
                dve.tensor_scalar(fx, fx, -float(np.float32(np.pi)), float(np.float32(np.pi)), ALU.max, ALU.min).then_inc(f_red, 1)
            for t in range(NT):
                dve.wait_ge(f_h, t + 1)
                for part in range(2):
                    ins = dve.tensor_tensor(taps[:, t, part * D:(part + 1) * D],
                                            ps[:, 4 + 2 * part:6 + 2 * part, :].rearrange("p a b -> p (a b)"),
                                            decay[:, t, :], ALU.mult)
                    if part == 0:
                        st.do(ins)
                ins.then_inc(f_taps, 1)
            dve.wait_ge(f_taps, NT)
            st.do(dve.memset(taps[0:1, 0, D:2 * D], 0.0))
            st.settle()
            st.do(dve.tensor_tensor(ytmp, taps[:, :, 0:D], taps[:, :, D:2 * D], ALU.add))
            st.settle()
            st.do(dve.tensor_tensor(taps[:, :, D:2 * D], taps[:, :, D:2 * D], taps[:, :, 0:D], ALU.subtract))
            st.settle()
            dve.tensor_copy(taps[:, :, 0:D], ytmp).then_inc(f_pm, 1)
            wall_at(dve, 3)

            norm("n_h", xs)
            for c in range(6):
                dve.wait_ge(bank_free, L_hin.e0 + c + 3)
                for j in range(4 * c, 4 * c + 4):
                    st.do(dve.tensor_scalar(zc[:, j, :], zT[:, j, :], hysw[:, j, 1:2], hysb[:, j:j + 1], ALU.mult, ALU.add))
                st.settle()
                for tap in (0, 2):
                    to = slice(1, T) if tap == 0 else slice(0, T - 1)
                    fr = slice(0, T - 1) if tap == 0 else slice(1, T)
                    for j in range(4 * c, 4 * c + 4):
                        st.do(dve.scalar_tensor_tensor(zc[:, j, to], zT[:, j, fr], hysw[:, j, tap:tap + 1], zc[:, j, to],
                                                       ALU.mult, ALU.add))
                    st.settle()
            x0, x1, vg = zc[:, 0:8, :], zc[:, 8:16, :], zc[:, 16:24, :]
            dve.tensor_tensor(vg, vg, x1, ALU.mult).then_inc(vv_ready, 1)
            dve.wait_ge(k_out, 4)
            kr, ki, vr, vs = Kf[:, 0], Kf[:, 1], Vf[:, 0], Vf[:, 1]
            st.do(dve.tensor_tensor(Yf[:, 0], vr, kr, ALU.mult))
            st.do(dve.tensor_tensor(ytmp, vs, ki, ALU.mult))
            st.settle()
            st.do(dve.tensor_tensor(Yf[:, 0], Yf[:, 0], ytmp, ALU.add))
            st.do(dve.tensor_tensor(Yf[:, 1], vs, kr, ALU.mult))
            st.settle()
            st.do(dve.tensor_tensor(ytmp, vr, ki, ALU.mult))
            st.settle()
            dve.tensor_tensor(Yf[:, 1], Yf[:, 1], ytmp, ALU.subtract).then_inc(y_freq, 1)
            dve.wait_ge(conv_mm, 1)
            for b in range(KT):
                st.do(dve.scalar_tensor_tensor(vg[:, b, :], vg[:, b, :], hyd[:, b:b + 1],
                                               ps[:, 4 + b // 2, (b % 2) * T:(b % 2 + 1) * T], ALU.mult, ALU.add))
            st.settle()
            dve.tensor_tensor(hT[:, :, :], vg, x0, ALU.mult).then_inc(vv_ready, 1)
            dve.wait_ge(vec_full, rows_in["o_1"])
            for c in range(2):
                cols = slice(c * CW, (c + 1) * CW)
                e = L_hout.e0 + c
                dve.wait_ge(ring_done, L_hout.g0 + c + 3)
                for t in range(NT):
                    ins = dve.tensor_tensor(yH[:, t, cols], ps[:, 2 * (e % 2) + t, :], vec[:, SHIFT, cols], ALU.add)
                    if t < NT - 1:
                        st.do(ins)
                ins.then_inc(bank_free, 1)
            dve.wait_ge(bank_free, L_hout.e0 + 2 + 2)
            post("o_1", yH)
            wall_at(dve, 4)
            mlp(1)
            wall_at(dve, 5)

        @block.gpsimd
        def _(pool):
            st = Steps(pool, pool_step)
            for dst, src in consts:
                pool.dma_start(dst, src).then_inc(consts_in, 16)

            def ask(p, t, K, u, col, i):
                n, hop = GROUP * (K + u), i * (SETS * GROUP)

                def row(buf, slot, table, s, used, full):
                    pool.wait_ge(used, hop + (n + s + 1))
                    pool.sem_inc(gathers_sent, 1)
                    at = bass.IndirectOffsetOnAxis(ap=row_no[:, u, s:s + 1], axis=0)
                    pool.indirect_dma_start(buf[:, slot, :], None, table, at).then_inc(full[slot], 16)

                def row_u(s):
                    row(ubuf, s, A["peer_u"], s, dot_done, u_full)

                def row_v(s):
                    row(vbuf, (u % 2) * GROUP + s, A["peer_v"], s, axpy_done, v_full)

                pool.wait_ge(dot_done, hop + (n + 1))
                pool.sem_inc(gathers_sent, 1)
                pool.tensor_copy(row_no[:, u, :], eidx[:, p % 2, t, bass.ds(hop + (col + u * GROUP), GROUP)]).then_inc(idx_ready, 1)
                pool.wait_ge(idx_ready, i * SETS + (K + u + 1))
                pool.sem_inc(gathers_sent, 1)
                for s in range(GROUP):
                    row_u(s)
                    if s > 0:
                        row_v(s - 1)
                row_v(GROUP - 1)

            def gathers(p):
                if p:
                    pool.wait_ge(peer_out, p)
                pool.dma_start(pgate[:, :], PEER_GATE[p].partition_broadcast(P)).then_inc(pgate_in, 16)
                for t in range(NT):
                    for q in range(PARTS):
                        pool.wait_ge(picks, PARTS * (NT * p + t) + q + 1)
                        K = ALLGRP * p + NGRP * t + q * (NGRP // PARTS)
                        with pool.Fori(0, NGRP // PARTS // SETS) as i:
                            for u in range(SETS):
                                ask(p, t, K, u, q * NQ, i)

            for s in range(2):
                pool.wait_ge(mod_stored[s], 16 * 7)
            for p in range(2):
                gathers(p)
            for s in range(2):
                pool.wait_ge(mod_stored[s], 16 * 13)
            gathers(2)
            wall_at(pool, 0)
            for dst, src in att_tabs:
                pool.dma_start(dst, src).then_inc(tab_in, 16)
            wall_at(pool, 1)
            wall_at(pool, 2)
            for dst, src in hy_tabs:
                pool.dma_start(dst, src).then_inc(tab_in, 16)
            for n in (3, 4, 5):
                wall_at(pool, n)
            pool.dma_start(out.rearrange("b (t p) d -> p (b t) d", p=P), xs[:, :, :]).then_inc(stored, 16)
            pool.wait_ge(stored, 16)


def tables():
    f32 = np.float32
    c = {"ident": np.eye(P, dtype=f32), "mean_mat": np.full((P, P), 1.0 / P, f32)}
    c["eps"] = np.full((P, 1), EPS, f32)
    s, t = np.meshgrid(np.arange(P), np.arange(P), indexing="ij")
    m = np.zeros((P, 14, P), f32)
    for lev in range(7):
        same = (s >> (lev + 1)) == (t >> (lev + 1))
        m[:, lev] = same & ((s >> lev) % 2 == 0) & ((t >> lev) % 2 == 1)
        m[:, 7 + lev] = same & ((s >> lev) % 2 == 1) & ((t >> lev) % 2 == 0)
    c["masks"] = m
    c["iota16"] = np.tile(np.arange(TOPK, dtype=f32), (P, 1))
    inv = f32(10000.0) ** (-np.arange(16, dtype=f32) / f32(16))
    pos = np.stack([np.arange(T) // GRID_W, np.arange(T) % GRID_W], 1).astype(f32)
    ang = pos[:, :, None] * inv[None, None, :].astype(f32)
    co, si = np.cos(ang).astype(f32), np.sin(ang).astype(f32)
    c["rope_cos"] = np.stack([co, co], 2).reshape(T, AD)
    c["rope_sin"] = np.stack([-si, si], 2).reshape(T, AD)
    n, f = np.meshgrid(np.arange(T), np.arange(T), indexing="ij")
    th = 2.0 * np.pi * ((n * (2 * f + 1)) % (4 * T)) / (4.0 * T)
    c["dft"] = np.stack([np.cos(th), np.sin(th)]).astype(f32)
    c["idft"] = (np.stack([np.cos(th).T, np.sin(th).T]) / T).astype(f32)
    bands = (EMB - 1) // 2
    tt = np.linspace(0.0, 1.0, T, dtype=f32)[:, None]
    w = (f32(2.0 * np.pi) * np.arange(T, dtype=f32)[:, None] / f32(T)).astype(f32)
    fr = np.linspace(1e-4, bands - 1, bands, dtype=f32)[None, :]
    arg = (fr * w).astype(f32)
    c["filt_emb"] = np.ascontiguousarray(np.concatenate([tt, np.cos(arg), -np.sin(arg)], 1).astype(f32).T)
    deltas = np.abs(np.linspace(np.log(1e-2) / 1.5, np.log(1e-2) / 0.3, D, dtype=f32))
    c["decay"] = np.exp(-tt * deltas[None, :]).astype(f32)
    return c


def lay_out(i):
    r = {}

    def blocks(v):
        return np.moveaxis(v.reshape((-1, P) + v.shape[1:]), 0, 1)

    r["x"], r["ctx"], r["ctx_2"] = i["x"][0], i["ctx"][0], i["ctx_2"][0]
    conds = np.stack([i["c"][0], i["c_ctx"], i["c_2"][0], i["c_ctx_2"]], 1)
    r["condT"] = blocks(conds)
    r["w_mod4"] = np.concatenate([i["w_mod"], i["w_mod_2"]])
    r["b_mod4"] = np.concatenate([i["b_mod"], i["b_mod_2"]])
    for k in ("norm1_g", "norm2_g", "final_g", "w_in", "w_out", "peer_wq"):
        r[k] = i[k]
    r["convT"] = np.stack([blocks(w.T) for w in i["conv_w"]], 1)
    lbl = i["lb_logits"]
    r["lbT"] = lbl.reshape(lbl.shape[0], 2, HEADS, P).transpose(3, 0, 1, 2)
    sk = i["peer_subkeys"]
    r["subkT"] = sk.transpose(0, 4, 1, 2, 3).reshape(sk.shape[0], P, 2 * PH, PK)
    r["peer_u"] = i["peer_u"].reshape(-1, D)
    r["peer_v"] = i["peer_v"].reshape(-1, D)
    for k in ("norm_mix_pre", "norm_mix_post", "norm_mlp_pre", "norm_mlp_post", "w_mlp_in", "w_mlp_out"):
        r[k] = i[k + "_2"]
    for k in ("attn_w_qkv", "attn_w_out", "attn_subln", "hy_w_in", "hy_w_out", "hy_b_out",
              "hy_filt_w1", "hy_filt_w2", "hy_filt_w_out"):
        r[k] = i[k + "_2"][0]
    r["attn_lambda"] = i["attn_lambda_2"][0].reshape(-1)
    r["filt_b"] = np.stack([i["hy_filt_b1_2"][0], *i["hy_filt_b2_2"][0], i["hy_filt_freq_2"][0]], 1)
    r["hy_bT"] = blocks(i["hy_b_in_2"][0])
    r["hy_swT"] = blocks(i["hy_w_short_2"][0].T)
    r["hy_sbT"] = blocks(i["hy_b_short_2"][0])
    r["hy_dT"] = blocks(i["hy_bias_2"][0])
    return r


def kernel(**inputs):
    import concourse.bacc as bacc
    from concourse.bass_utils import run_bass_kernel_spmd

    nc = bacc.Bacc("TRN2", target_bir_lowering=False, num_devices=1)
    given = {k: np.asarray(v) for k, v in inputs.items()}
    arrays, A = {}, {}
    for name, v in {**lay_out(given), **tables()}.items():
        v = np.ascontiguousarray(v)
        arrays["in_" + name] = v
        A[name] = nc.dram_tensor("in_" + name, v.shape, mybir.dt.from_np(v.dtype), kind="ExternalInput").ap()
    out = nc.dram_tensor("out", (1, T, D), F32, kind="ExternalOutput").ap()
    program(nc, A, out)
    got = run_bass_kernel_spmd(nc, [arrays], core_ids=[0])
    return got.results[0]["out"]
```
